# Optimizing a Trainium2 kernel written in Bass

```python
import math
import jax
import jax.numpy as jnp
from jax import lax
import numpy as np

D_MODEL = 1024
BATCH = 1
SEQ = 128
DEPTH = 2
DEC_BATCH = 1
DEC_SEQ = 512
PAST_LEN = 128

GRID_W = 64
N_EVEN = (DEPTH + 1) // 2
N_ODD = DEPTH // 2
RWKV_HEADS = 12
HEAD_SIZE = 64
D_RWKV = RWKV_HEADS * HEAD_SIZE
DECAY_LORA = 64
AAA_LORA = 64
GATE_LORA = 128
GN_EPS = 64e-5
FNET_GROUPS = 4
FNET_GROUP_W = 64
D_FNET = FNET_GROUPS * FNET_GROUP_W
D_SHIFTED = 3 * D_RWKV + 2 * DECAY_LORA + 2 * AAA_LORA + GATE_LORA
D_AB_IN = D_SHIFTED + D_FNET
HY_BANDS = 16
HY_EMB = 2 * HY_BANDS + 1
HY_ORDER = 64
PEER_HEADS = 8
N_KEYS = 128
N_EXPERTS = N_KEYS * N_KEYS
PEER_DK = 256
PEER_TOPK = 16
PEER_BLOCK = 128
LN_EPS = 1e-5
DN_ALPHA = (2 * DEPTH) ** 0.25
DN_BETA = (8 * DEPTH) ** -0.25

kernel_name = 'hybrid_rwkv7_fnet_hyena_peer_prefix_step'

F32 = jnp.float32

def layer_norm(x, g=None, b=None):
    xf = x.astype(F32)
    mu = jnp.mean(xf, axis=-1, keepdims=True)
    var = jnp.mean(jnp.square(xf - mu), axis=-1, keepdims=True)
    y = (xf - mu) * lax.rsqrt(var + LN_EPS)
    if g is not None:
        y = y * g.astype(F32) + b.astype(F32)
    return y.astype(x.dtype)

def shift_prev(z):
    return jnp.pad(z, ((0, 0), (1, 0), (0, 0)))[:, :-1]

def shift_next(z):
    return jnp.pad(z, ((0, 0), (0, 1), (0, 0)))[:, 1:]

def modulation(cvec, w_mod, b_mod):
    m = jax.nn.silu(cvec) @ w_mod + b_mod
    return jnp.split(m, 6, axis=-1)

def grid_pos_embed(n_tokens):
    rows = n_tokens // GRID_W
    row = jnp.repeat(jnp.arange(rows, dtype=F32), GRID_W)
    col = jnp.tile(jnp.arange(GRID_W, dtype=F32), rows)
    quarter = D_MODEL // 4
    omega = 1.0 / (10000.0 ** (jnp.arange(quarter, dtype=F32) / quarter))
    ra = row[:, None] * omega[None, :]
    ca = col[:, None] * omega[None, :]
    return jnp.concatenate([jnp.sin(ra), jnp.cos(ra), jnp.sin(ca), jnp.cos(ca)], axis=-1)

def wkv7_scan(r, decay, k, v, kk, a, s0, reverse):
    def step(s, inp):
        r_t, w_t, k_t, v_t, kk_t, a_t = inp
        sa = jnp.einsum('bhij,bhj->bhi', s, -kk_t)
        s = (s * w_t[:, :, None, :]
             + sa[..., None] * (kk_t * a_t)[:, :, None, :]
             + v_t[..., None] * k_t[:, :, None, :])
        return s, jnp.einsum('bhij,bhj->bhi', s, r_t)
    xs = tuple(jnp.swapaxes(t, 0, 1) for t in (r, decay, k, v, kk, a))
    s_fin, ys = lax.scan(step, s0, xs, reverse=reverse)
    return jnp.swapaxes(ys, 0, 1), s_fin

def rwkv_mix(zs, e, P, s0_f, s0_b):
    B, L, _ = zs.shape
    splits = [D_RWKV, 2 * D_RWKV, 3 * D_RWKV,
              3 * D_RWKV + DECAY_LORA, 3 * D_RWKV + 2 * DECAY_LORA,
              3 * D_RWKV + 2 * DECAY_LORA + AAA_LORA, 3 * D_RWKV + 2 * DECAY_LORA + 2 * AAA_LORA]
    r, k, v, zw_f, zw_b, za_f, za_b, zg = jnp.split(zs, splits, axis=-1)

    def heads(t):
        return t.astype(F32).reshape(B, L, RWKV_HEADS, HEAD_SIZE)

    r_h, k_h, v_h = heads(r), heads(k), heads(v)
    kk = heads(k * P['rwkv_k_k'][e])
    kk = kk * lax.rsqrt(jnp.sum(kk * kk, axis=-1, keepdims=True) + 1e-12)
    k_a = P['rwkv_k_a'][e].astype(F32).reshape(RWKV_HEADS, HEAD_SIZE)
    ys, finals, k_dirs = [], [], []
    for d, (zw, za, s0, rev) in enumerate(((zw_f, za_f, s0_f, False), (zw_b, za_b, s0_b, True))):
        w_raw = (P['rwkv_w0'][e, d] + jnp.tanh(zw) @ P['rwkv_w2'][e, d]).astype(F32)
        decay = heads(jnp.exp(-jnp.exp(-jax.nn.softplus(-w_raw) - 0.5)))
        a = heads(jax.nn.sigmoid((P['rwkv_a0'][e, d] + za @ P['rwkv_a2'][e, d]).astype(F32)))
        k_d = k_h * (1.0 + (a - 1.0) * k_a)
        y_d, s_d = wkv7_scan(r_h, decay, k_d, v_h, kk, a, s0.astype(F32), rev)
        ys.append(y_d)
        finals.append(s_d)
        k_dirs.append(k_d)
    y = ys[0] + ys[1]
    mu = jnp.mean(y, axis=-1, keepdims=True)
    var = jnp.mean(jnp.square(y - mu), axis=-1, keepdims=True)
    y = ((y - mu) * lax.rsqrt(var + GN_EPS)).reshape(B, L, D_RWKV)
    y = y * P['rwkv_gn_g'][e].astype(F32) + P['rwkv_gn_b'][e].astype(F32)
    k_bonus = 0.5 * (k_dirs[0] + k_dirs[1])
    bonus = jnp.sum(r_h * k_bonus * P['rwkv_r_k'][e].astype(F32), axis=-1, keepdims=True) * v_h
    y = y + bonus.reshape(B, L, D_RWKV)
    g = jax.nn.sigmoid(zg) @ P['rwkv_g2'][e]
    return y.astype(zs.dtype) * g, finals[0], finals[1]

def fourier_mix(zf):
    B, L, _ = zf.shape
    z = zf.astype(F32).reshape(B, L, FNET_GROUPS, FNET_GROUP_W)
    y = jnp.fft.fft2(z, axes=(1, 3), norm='ortho').real
    return y.reshape(B, L, D_FNET).astype(zf.dtype)

def ab_mixer(h, e, P, s0_f, s0_b):
    z = h @ P['ab_w_in'][e]
    zs, zf = z[..., :D_SHIFTED], z[..., D_SHIFTED:]
    zs = zs + P['ab_mu'][e] * (0.5 * (shift_prev(zs) + shift_next(zs)) - zs)
    y_a, s_f, s_b = rwkv_mix(zs, e, P, s0_f, s0_b)
    y_b = fourier_mix(zf)
    y = jnp.concatenate([y_a, y_b], axis=-1) @ P['ab_w_out'][e]
    return y, s_f, s_b

def hyena_filters(L, w1, b1, w2, b2, w3, freq, decay):
    pos = jnp.arange(L, dtype=F32)[:, None]
    t = pos / (L - 1)
    bands = jnp.linspace(1e-4, HY_BANDS - 1, HY_BANDS, dtype=F32)[None, :]
    ang = 2.0 * math.pi * pos / L * bands
    feats = jnp.concatenate([t, jnp.cos(ang), -jnp.sin(ang)], axis=-1)
    fr = freq.astype(F32)
    hid = jnp.sin(fr * (feats @ w1.astype(F32) + b1.astype(F32)))
    hid = jnp.sin(fr * (hid @ w2.astype(F32) + b2.astype(F32)))
    filt = (hid @ w3.astype(F32)) * jnp.exp(-t * jnp.abs(decay.astype(F32)))
    return filt[:, :D_MODEL], filt[:, D_MODEL:]

def long_conv(u, h_f, h_b, skip):
    L, D = h_f.shape
    taps = jnp.concatenate([h_f, jnp.zeros((1, D), F32), h_b[:0:-1]], axis=0)
    uf = jnp.fft.rfft(u, n=2 * L, axis=1)
    tf = jnp.fft.rfft(taps, axis=0)
    y = jnp.fft.irfft(uf * tf[None], n=2 * L, axis=1)[:, :L]
    return y + u * skip

def hyena_mixer(h, o, P):
    L = h.shape[1]
    z = h @ P['hy_w_in'][o]
    cw = P['hy_conv_w'][o]
    z = cw[0] * shift_prev(z) + cw[1] * z + cw[2] * shift_next(z) + P['hy_conv_b'][o]
    x0, x1, v = jnp.split(z, 3, axis=-1)
    h_f, h_b = hyena_filters(L, P['hy_filt_w1'][o], P['hy_filt_b1'][o], P['hy_filt_w2'][o],
                             P['hy_filt_b2'][o], P['hy_filt_w3'][o], P['hy_filt_freq'][o],
                             P['hy_filt_decay'][o])
    y = long_conv((v * x1).astype(F32), h_f, h_b, P['hy_skip'][o].astype(F32))
    return (y.astype(h.dtype) * x0) @ P['hy_w_out'][o]

def peer(h, layer, P):
    B, L, D = h.shape
    T = B * L
    x = h.reshape(T, D)
    q = (x @ P['peer_wq'][layer]).astype(F32).reshape(T, PEER_HEADS, 2, PEER_DK // 2)
    s1 = jnp.einsum('thd,hnd->thn', q[:, :, 0], P['peer_k1'][layer].astype(F32))
    s2 = jnp.einsum('thd,hnd->thn', q[:, :, 1], P['peer_k2'][layer].astype(F32))
    v1, i1 = lax.top_k(s1, PEER_TOPK)
    v2, i2 = lax.top_k(s2, PEER_TOPK)
    n_cand = PEER_TOPK * PEER_TOPK
    cand = (v1[..., :, None] + v2[..., None, :]).reshape(T, PEER_HEADS, n_cand)
    cidx = (i1[..., :, None] * N_KEYS + i2[..., None, :]).reshape(T, PEER_HEADS, n_cand)
    best, pos = lax.top_k(cand, PEER_TOPK)
    idx = jnp.take_along_axis(cidx, pos, axis=-1)
    gates = jax.nn.softmax(best, axis=-1).astype(h.dtype)
    n_blk = T // PEER_BLOCK
    n_sel = PEER_HEADS * PEER_TOPK
    u_tab = P['peer_u'][layer]
    v_tab = P['peer_v'][layer]

    def expert_block(args):
        xb, ib, gb = args
        act = jax.nn.gelu(jnp.einsum('td,ted->te', xb, u_tab[ib])) * gb
        return jnp.einsum('te,ted->td', act, v_tab[ib])

    out = lax.map(expert_block, (x.reshape(n_blk, PEER_BLOCK, D),
                                 idx.reshape(n_blk, PEER_BLOCK, n_sel),
                                 gates.reshape(n_blk, PEER_BLOCK, n_sel)))
    return out.reshape(B, L, D)

def run_layer(layer, x, cvec, s0_f, s0_b, P):
    sh1, sc1, g1, sh2, sc2, g2 = modulation(cvec, P['w_mod'][layer], P['b_mod'][layer])
    h = layer_norm(x) * (1.0 + sc1) + sh1
    if layer % 2 == 0:
        y, s_f, s_b = ab_mixer(h, layer // 2, P, s0_f, s0_b)
    else:
        y = hyena_mixer(h, layer // 2, P)
        s_f, s_b = None, None
    x = layer_norm(DN_ALPHA * x + g1 * y, P['ln_mix_g'][layer], P['ln_mix_b'][layer])
    h = layer_norm(x) * (1.0 + sc2) + sh2
    y = peer(h, layer, P)
    x = layer_norm(DN_ALPHA * x + g2 * y, P['ln_ffn_g'][layer], P['ln_ffn_b'][layer])
    return x, s_f, s_b

def setup_inputs(seed: int = 0) -> dict:
    key = jax.random.key(seed)
    keys = iter(jax.random.split(key, 48))

    def nrm(shape, std):
        return std * jax.random.normal(next(keys), shape, F32)

    D = D_MODEL
    st_shape = (DEC_BATCH, N_EVEN, RWKV_HEADS, HEAD_SIZE, HEAD_SIZE)
    return {
        'x_prompt': nrm((BATCH, SEQ, D), 1.0),
        'x_sample': nrm((DEC_BATCH, DEC_SEQ, D), 1.0),
        'c': nrm((DEC_BATCH, D), 1.0),
        'state_rwkv_fwd': nrm(st_shape, 0.5),
        'state_rwkv_bwd': nrm(st_shape, 0.5),
        'c_ctx': nrm((D,), 1.0),
        'w_mod': nrm((DEPTH, D, 6 * D), 0.5 * D ** -0.5),
        'b_mod': nrm((DEPTH, 6 * D), 0.02),
        'ln_mix_g': 1.0 + nrm((DEPTH, D), 0.02),
        'ln_mix_b': nrm((DEPTH, D), 0.02),
        'ln_ffn_g': 1.0 + nrm((DEPTH, D), 0.02),
        'ln_ffn_b': nrm((DEPTH, D), 0.02),
        'peer_wq': nrm((DEPTH, D, PEER_HEADS * PEER_DK), D ** -0.5),
        'peer_k1': nrm((DEPTH, PEER_HEADS, N_KEYS, PEER_DK // 2), (PEER_DK // 2) ** -0.5),
        'peer_k2': nrm((DEPTH, PEER_HEADS, N_KEYS, PEER_DK // 2), (PEER_DK // 2) ** -0.5),
        'peer_u': nrm((DEPTH, N_EXPERTS, D), D ** -0.5),
        'peer_v': nrm((DEPTH, N_EXPERTS, D), DN_BETA),
        'ab_w_in': nrm((N_EVEN, D, D_AB_IN), D ** -0.5),
        'ab_mu': jax.random.uniform(next(keys), (N_EVEN, D_SHIFTED), F32, 0.2, 0.8),
        'rwkv_w0': -1.0 + nrm((N_EVEN, 2, D_RWKV), 0.5),
        'rwkv_w2': nrm((N_EVEN, 2, DECAY_LORA, D_RWKV), 0.5 * DECAY_LORA ** -0.5),
        'rwkv_a0': nrm((N_EVEN, 2, D_RWKV), 0.5),
        'rwkv_a2': nrm((N_EVEN, 2, AAA_LORA, D_RWKV), 0.5 * AAA_LORA ** -0.5),
        'rwkv_g2': nrm((N_EVEN, GATE_LORA, D_RWKV), GATE_LORA ** -0.5),
        'rwkv_k_k': 1.0 + nrm((N_EVEN, D_RWKV), 0.1),
        'rwkv_k_a': 1.0 + nrm((N_EVEN, D_RWKV), 0.1),
        'rwkv_r_k': nrm((N_EVEN, RWKV_HEADS, HEAD_SIZE), 0.1),
        'rwkv_gn_g': 1.0 + nrm((N_EVEN, D_RWKV), 0.02),
        'rwkv_gn_b': nrm((N_EVEN, D_RWKV), 0.02),
        'ab_w_out': nrm((N_EVEN, D, D), DN_BETA * D ** -0.5),
        'hy_w_in': nrm((N_ODD, D, 3 * D), D ** -0.5),
        'hy_conv_w': nrm((N_ODD, 3, 3 * D), 0.5),
        'hy_conv_b': nrm((N_ODD, 3 * D), 0.02),
        'hy_filt_w1': nrm((N_ODD, HY_EMB, HY_ORDER), HY_EMB ** -0.5),
        'hy_filt_b1': nrm((N_ODD, HY_ORDER), 0.1),
        'hy_filt_w2': nrm((N_ODD, HY_ORDER, HY_ORDER), HY_ORDER ** -0.5),
        'hy_filt_b2': nrm((N_ODD, HY_ORDER), 0.1),
        'hy_filt_w3': nrm((N_ODD, HY_ORDER, 2 * D), 0.1 * HY_ORDER ** -0.5),
        'hy_filt_freq': 1.0 + nrm((N_ODD, HY_ORDER), 0.05),
        'hy_filt_decay': jnp.tile(jnp.linspace(3.07, 15.35, D, dtype=F32), 2)[None, :] * (1.0 + nrm((N_ODD, 2 * D), 0.05)),
        'hy_skip': nrm((N_ODD, D), 0.5),
        'hy_w_out': nrm((N_ODD, D, D), DN_BETA * D ** -0.5),
    }

def reference(x_prompt, x_sample, c, state_rwkv_fwd, state_rwkv_bwd, c_ctx,
              w_mod, b_mod, ln_mix_g, ln_mix_b, ln_ffn_g, ln_ffn_b,
              peer_wq, peer_k1, peer_k2, peer_u, peer_v,
              ab_w_in, ab_mu, rwkv_w0, rwkv_w2, rwkv_a0, rwkv_a2, rwkv_g2,
              rwkv_k_k, rwkv_k_a, rwkv_r_k, rwkv_gn_g, rwkv_gn_b, ab_w_out,
              hy_w_in, hy_conv_w, hy_conv_b, hy_filt_w1, hy_filt_b1, hy_filt_w2,
              hy_filt_b2, hy_filt_w3, hy_filt_freq, hy_filt_decay, hy_skip, hy_w_out):
    P = {
        'w_mod': w_mod, 'b_mod': b_mod,
        'ln_mix_g': ln_mix_g, 'ln_mix_b': ln_mix_b, 'ln_ffn_g': ln_ffn_g, 'ln_ffn_b': ln_ffn_b,
        'peer_wq': peer_wq, 'peer_k1': peer_k1, 'peer_k2': peer_k2, 'peer_u': peer_u, 'peer_v': peer_v,
        'ab_w_in': ab_w_in, 'ab_mu': ab_mu, 'rwkv_w0': rwkv_w0, 'rwkv_w2': rwkv_w2,
        'rwkv_a0': rwkv_a0, 'rwkv_a2': rwkv_a2, 'rwkv_g2': rwkv_g2, 'rwkv_k_k': rwkv_k_k,
        'rwkv_k_a': rwkv_k_a, 'rwkv_r_k': rwkv_r_k, 'rwkv_gn_g': rwkv_gn_g, 'rwkv_gn_b': rwkv_gn_b,
        'ab_w_out': ab_w_out,
        'hy_w_in': hy_w_in, 'hy_conv_w': hy_conv_w, 'hy_conv_b': hy_conv_b,
        'hy_filt_w1': hy_filt_w1, 'hy_filt_b1': hy_filt_b1, 'hy_filt_w2': hy_filt_w2,
        'hy_filt_b2': hy_filt_b2, 'hy_filt_w3': hy_filt_w3, 'hy_filt_freq': hy_filt_freq,
        'hy_filt_decay': hy_filt_decay, 'hy_skip': hy_skip, 'hy_w_out': hy_w_out,
    }
    x_ctx = x_prompt
    c_ctx_vec = c_ctx[None, None, :]
    zero_state = jnp.zeros((x_prompt.shape[0], RWKV_HEADS, HEAD_SIZE, HEAD_SIZE), F32)
    x_lat = x_sample + grid_pos_embed(x_sample.shape[1]).astype(x_sample.dtype)
    c_lat_vec = c[:, None, :]
    new_f, new_b = [], []
    for layer in range(DEPTH):
        x_ctx, s_f, s_b = run_layer(layer, x_ctx, c_ctx_vec, zero_state, zero_state, P)
        if layer % 2 == 0:
            e = layer // 2
            new_f.append(s_f)
            new_b.append(s_b)
            x_lat, _, _ = run_layer(layer, x_lat, c_lat_vec,
                                    state_rwkv_fwd[:, e], state_rwkv_bwd[:, e], P)
        else:
            x_lat, _, _ = run_layer(layer, x_lat, c_lat_vec, None, None, P)
    y_prompt = x_ctx
    y_sample = x_lat
    new_state_rwkv_fwd = jnp.stack(new_f, axis=1)
    new_state_rwkv_bwd = jnp.stack(new_b, axis=1)
    return (y_prompt, y_sample, new_state_rwkv_fwd, new_state_rwkv_bwd)


_drawn_inputs = setup_inputs


def setup_inputs(seed=0):
    import zlib

    import numpy as np

    out = dict(_drawn_inputs(seed))
    spreads = {}
    factors = {'state_rwkv_fwd': 8.0,
     'state_rwkv_bwd': 8.0,
     'rwkv_r_k': 4.188,
     'rwkv_gn_g': 8.0,
     'rwkv_gn_b': 8.0,
     'hy_conv_b': 8.0,
     'hy_filt_b1': 4.996,
     'hy_filt_b2': 3.441,
     'hy_filt_freq': 8.0}
    for name, (base, spread) in spreads.items():
        noise = np.random.default_rng([zlib.crc32(name.encode()), seed]).standard_normal(out[name].shape)
        drawn = base * np.exp(spread * noise) if base else spread * noise
        out[name] = jnp.asarray(drawn.astype(out[name].dtype))
    for name, factor in factors.items():
        out[name] = (out[name] * factor).astype(out[name].dtype)
    return out
```

```python
from contextlib import ExitStack

import numpy as np

import concourse.bass as bass
from concourse import mybir

ALU = mybir.AluOpType
ACT = mybir.ActivationFunctionType
F32 = mybir.dt.float32
F32R = mybir.dt.float32r
U32 = mybir.dt.uint32

P = 128
D = 1024
KD = D // P
T_CTX, T_LAT = 128, 512
T = T_CTX + T_LAT
TT = T // P
SEGS = [(0, 0, T_CTX), (1, T_CTX, T_LAT)]
BANK = 512
DEPTH = 2
ALPHA = float((2 * DEPTH) ** 0.25)
LN_EPS = 1e-5
GN_EPS = 64e-5
HEADS, HS = 12, 64
PAIRS = HEADS // 2
CH = 64
LEVELS = 6
DECAY_C = float(np.exp(-0.5))
GRID_W = 64
MOD_TILES = DEPTH * 6 * D // BANK
ZW = 1 + T_CTX + 2 + T_LAT + 1
ZOFF = [1, T_CTX + 3]
(PC_MU_R, PC_MU_K, PC_MU_V, PC_KK, PC_KA, PC_RK, PC_GNG, PC_GNB, PC_W0, PC_W0B, PC_A0, PC_A0B) = range(12)
NPC = 12


class Shared:
    pass


def linker(eng, sem):
    count = [0]

    def link(ins):
        count[0] += 1
        ins.then_inc(sem, 1)
        eng.wait_ge(sem, count[0])
    return link


def clear(nc, s):
    with nc.Block() as block:
        @block.gpsimd
        def _(pool):
            for x in s.values():
                pool.sem_clear(x)


def sems(ctx, nc, *names):
    s = {n: ctx.enter_context(nc.semaphore(f"{n}_{nc.next_id()}")) for n in names}
    ctx.callback(clear, nc, s)
    return s


def buf(ctx, nc, name, *shape, dtype=F32):
    return ctx.enter_context(nc.sbuf_tensor(f"{name}_{nc.next_id()}", list(shape), dtype))


def load_inputs(nc, m):
    with ExitStack() as ctx:
        pos = buf(ctx, nc, "pos", P, TT - 1, D)
        s = sems(ctx, nc, "li_tokens", "li_pos", "li_const", "li_sum")
        with nc.Block() as block:
            @block.sync
            def _(sp):
                sp.dma_start(m.x[:, 0, :], m.i["x_prompt"]).then_inc(s["li_tokens"], 16)
                sp.dma_start(m.x[:, 1:TT, :], m.i["x_sample"].rearrange("(t p) d -> p t d", p=P)).then_inc(s["li_tokens"], 16)
                sp.dma_start(pos[:, :, :], m.i["pos"].rearrange("(t p) d -> p t d", p=P)).then_inc(s["li_pos"], 16)
                sp.dma_start(m.ident[:, :], m.i["ident"]).then_inc(s["li_const"], 16)
                sp.dma_start(m.eps[:, :], m.i["eps"]).then_inc(s["li_const"], 16)
                sp.dma_start(m.iota[:, :], m.i["iota"]).then_inc(s["li_const"], 16)
                sp.wait_ge(s["li_const"], 48)

            @block.vector
            def _(dve):
                dve.wait_ge(s["li_tokens"], 32)
                dve.wait_ge(s["li_pos"], 16)
                dve.tensor_tensor(m.x[:, 1:TT, :], m.x[:, 1:TT, :], pos[:, :, :], ALU.add).then_inc(s["li_sum"], 1)
                dve.wait_ge(s["li_sum"], 1)


def modulation(nc, m):
    with ExitStack() as ctx:
        c_in = buf(ctx, nc, "c_in", P, KD, 2)
        c_act = buf(ctx, nc, "c_act", P, KD, 2)
        w = buf(ctx, nc, "w_modt", P, 4, KD, BANK)
        row = buf(ctx, nc, "mod_row", 2, MOD_TILES * BANK)
        bias = buf(ctx, nc, "mod_bias", 2, MOD_TILES * BANK)
        s = sems(ctx, nc, "mo_c", "mo_bias", "mo_w0", "mo_w1", "mo_w2", "mo_w3", "mo_silu", "mo_mm", "mo_row", "mo_tr", "mo_col", "mo_out", "mo_plus")
        landed = [s["mo_w0"], s["mo_w1"], s["mo_w2"], s["mo_w3"]]
        NT = MOD_TILES
        with nc.Block() as block:
            @block.sync
            def _(sp):
                sp.dma_start(c_in[:, :, :], m.i["cond"]).then_inc(s["mo_c"], 16)
                sp.dma_start(bias[:, :], m.i["b_mod"].partition_broadcast(2)).then_inc(s["mo_bias"], 16)
                for n in range(NT):
                    if n >= 4:
                        sp.wait_ge(s["mo_mm"], n - 3)
                    sp.dma_start(w[:, n % 4, :, :], m.i["w_mod"][n]).then_inc(landed[n % 4], 16)
                sp.wait_ge(s["mo_row"], NT)
                sp.dma_start(m.mods, row[:, :]).then_inc(s["mo_out"], 16)
                sp.wait_ge(s["mo_out"], 16)

            @block.scalar
            def _(act):
                act.wait_ge(s["mo_c"], 16)
                act.activation(c_act[:, :, :], c_in[:, :, :], ACT.Silu).then_inc(s["mo_silu"], 1)

            @block.tensor
            def _(pe):
                pe.wait_ge(s["mo_silu"], 1)
                for n in range(NT):
                    pe.wait_ge(landed[n % 4], 16 * (n // 4 + 1))
                    if n >= 4:
                        pe.wait_ge(s["mo_row"], n - 3)
                    for k in range(KD):
                        mm = pe.matmul(m.bank[n % 4][0:2, :], c_act[:, k, :], w[:, n % 4, k, :], start=(k == 0), stop=(k == KD - 1))
                    mm.then_inc(s["mo_mm"], 1)
                pe.wait_ge(s["mo_row"], NT)
                for j in range(NT * 4):
                    mm = pe.transpose(m.bank[4][:, 2 * j:2 * j + 2], row[:, j * P:(j + 1) * P], m.ident[0:2, 0:2])
                mm.then_inc(s["mo_tr"], 1)

            @block.vector
            def _(dve):
                dve.wait_ge(s["mo_bias"], 16)
                for n in range(NT):
                    dve.wait_ge(s["mo_mm"], n + 1)
                    dve.tensor_tensor(row[:, n * BANK:(n + 1) * BANK], m.bank[n % 4][0:2, :], bias[:, n * BANK:(n + 1) * BANK],
                                      ALU.add).then_inc(s["mo_row"], 1)
                dve.wait_ge(s["mo_tr"], 1)
                dve.tensor_copy(m.modc[:, :], m.bank[4][:, 0:NT * 8]).then_inc(s["mo_col"], 1)
                dve.wait_ge(s["mo_col"], 1)
                for layer in range(DEPTH):
                    for j in (1, 4):
                        a = (layer * 6 + j) * KD * 2
                        dve.tensor_scalar(m.modc[:, a:a + KD * 2], m.modc[:, a:a + KD * 2], 1.0, None, ALU.add).then_inc(s["mo_plus"], 1)
                dve.wait_ge(s["mo_plus"], 4)


def mod_col(m, layer, j, k, cond):
    a = ((layer * 6 + j) * KD + k) * 2 + cond
    return m.modc[:, a:a + 1]


def norm_modulate(nc, m, layer, sub):
    with ExitStack() as ctx:
        xn = buf(ctx, nc, "xn", P, TT, D)
        st = buf(ctx, nc, "st", P, TT, 2, 6)
        mv = buf(ctx, nc, "mv", P, TT, 2)
        sd = buf(ctx, nc, "sd", P, TT)
        rs = buf(ctx, nc, "rs", P, TT)
        s = sems(ctx, nc, "nm_chain", "nm_var", "nm_sd", "nm_xn", "nm_tr", "nm_dve", "nm_act", "nm_stat")
        with nc.Block() as block:
            @block.vector
            def _(dve):
                link = linker(dve, s["nm_chain"])
                for t in range(TT):
                    for h in range(2):
                        ins = dve.bn_stats(st[:, t, h, :], m.x[:, t, h * BANK:(h + 1) * BANK])
                    ins.then_inc(s["nm_stat"], 1)
                for t in range(TT):
                    dve.wait_ge(s["nm_stat"], t + 1)
                    ins = dve.bn_aggr(mv[:, t, :], st[:, t, :, :].rearrange("p a b -> p (a b)"))
                ins.then_inc(s["nm_var"], 1)
                dve.wait_ge(s["nm_sd"], 1)
                link(dve.reciprocal(rs[:, :], sd[:, :]))
                for t in range(TT):
                    dve.tensor_scalar(xn[:, t, :], m.x[:, t, :], mv[:, t, 0:1], rs[:, t:t + 1], ALU.subtract, ALU.mult).then_inc(s["nm_xn"], 1)
                for k in range(KD):
                    c, n = (1, T_LAT) if k % 2 == 0 else (0, T_CTX)
                    a = SEGS[c][1]
                    dve.wait_ge(s["nm_tr"], k + 1)
                    dve.tensor_scalar(m.hT[:, k, a:a + n], m.bank[k % 4 * 2 + c][:, 0:n], mod_col(m, layer, 3 * sub + 1, k, c),
                                      mod_col(m, layer, 3 * sub, k, c), ALU.mult, ALU.add).then_inc(s["nm_dve"], 1)
                dve.wait_ge(s["nm_dve"], KD)

            @block.scalar
            def _(act):
                act.wait_ge(s["nm_var"], 1)
                act.activation(sd[:, :], mv[:, :, 1], ACT.Sqrt, bias=m.eps[:, 0:1]).then_inc(s["nm_sd"], 1)
                for k in range(KD):
                    c, n = (0, T_CTX) if k % 2 == 0 else (1, T_LAT)
                    a = SEGS[c][1]
                    act.wait_ge(s["nm_tr"], k + 1)
                    act.activation(m.hT[:, k, a:a + n], m.bank[k % 4 * 2 + c][:, 0:n], ACT.Identity,
                                   scale=mod_col(m, layer, 3 * sub + 1, k, c),
                                   bias=mod_col(m, layer, 3 * sub, k, c)).then_inc(s["nm_act"], 1)
                act.wait_ge(s["nm_act"], KD)

            @block.tensor
            def _(pe):
                pe.wait_ge(s["nm_xn"], TT)
                for k in range(KD):
                    if k >= 4:
                        pe.wait_ge(s["nm_dve"], k - 3)
                        pe.wait_ge(s["nm_act"], k - 3)
                    pe.transpose(m.bank[k % 4 * 2][:, 0:P], xn[:, 0, k * P:(k + 1) * P], m.ident[:, :])
                    for t in range(1, TT):
                        mm = pe.transpose(m.bank[k % 4 * 2 + 1][:, (t - 1) * P:t * P], xn[:, t, k * P:(k + 1) * P], m.ident[:, :])
                    mm.then_inc(s["nm_tr"], 1)


def add_and_norm(nc, m, layer, sub, w_out=None, y=None):
    gam, bet = (m.i["ln_mix_g"], m.i["ln_mix_b"]) if sub == 0 else (m.i["ln_ffn_g"], m.i["ln_ffn_b"])
    with ExitStack() as ctx:
        gate = buf(ctx, nc, "gate", P, 2, D)
        gb = buf(ctx, nc, "gb", P, 2, D)
        tmp = buf(ctx, nc, "tmp", P, 2, D)
        st = buf(ctx, nc, "st", P, TT, 2, 6)
        mv = buf(ctx, nc, "mv", P, TT, 2)
        sd = buf(ctx, nc, "sd", P, TT)
        sh = buf(ctx, nc, "sh", P, TT)
        rs = buf(ctx, nc, "rs", P, TT)
        wo = buf(ctx, nc, "wo", P, KD, D) if w_out is not None else None
        s = sems(ctx, nc, "an_w", "an_rows", "an_chain", "an_mm", "an_free", "an_var", "an_sd", "an_shift", "an_norm", "an_scaled", "an_x")
        with nc.Block() as block:
            @block.sync
            def _(sp):
                if w_out is not None:
                    sp.dma_start(wo[:, :, :], w_out.rearrange("(k p) n -> p k n", p=P)).then_inc(s["an_w"], 16)
                for c in range(2):
                    a = (layer * 6 + 3 * sub + 2) * D
                    sp.dma_start(gate[:, c, :], m.mods[c, a:a + D].partition_broadcast(P)).then_inc(s["an_rows"], 16)
                sp.dma_start(gb[:, 0, :], gam[layer].partition_broadcast(P)).then_inc(s["an_rows"], 16)
                sp.dma_start(gb[:, 1, :], bet[layer].partition_broadcast(P)).then_inc(s["an_rows"], 16)

            if w_out is not None:
                @block.tensor
                def _(pe):
                    pe.wait_ge(s["an_w"], 16)
                    for t in range(TT):
                        for h in range(2):
                            n = 2 * t + h
                            if n >= 8:
                                pe.wait_ge(s["an_free"], n - 7)
                            for k in range(KD):
                                mm = pe.matmul(m.bank[n % 8][:, :], m.yT[:, k, t * P:(t + 1) * P], wo[:, k, h * BANK:(h + 1) * BANK],
                                               start=(k == 0), stop=(k == KD - 1))
                            mm.then_inc(s["an_mm"], 1)

            @block.scalar
            def _(act):
                for t in range(TT):
                    act.wait_ge(s["an_var"], t + 1)
                    act.activation(sd[:, t:t + 1], mv[:, t, 1:2], ACT.Sqrt, bias=m.eps[:, 0:1]).then_inc(s["an_sd"], 1)
                    act.wait_ge(s["an_shift"], t + 1)
                    act.activation(m.x[:, t, :], m.x[:, t, :], ACT.Identity, scale=rs[:, t:t + 1], bias=sh[:, t:t + 1]).then_inc(s["an_norm"], 1)

            @block.gpsimd
            def _(pool):
                pool.wait_ge(s["an_rows"], 64)
                for t in range(TT):
                    pool.wait_ge(s["an_norm"], t + 1)
                    pool.tensor_tensor(m.x[:, t, :], m.x[:, t, :], gb[:, 0, :], ALU.mult).then_inc(s["an_scaled"], 1)
                    pool.wait_ge(s["an_scaled"], t + 1)
                    pool.tensor_tensor(m.x[:, t, :], m.x[:, t, :], gb[:, 1, :], ALU.add).then_inc(s["an_x"], 1)
                pool.wait_ge(s["an_x"], TT)

            @block.vector
            def _(dve):
                link = linker(dve, s["an_chain"])

                def scale_and_shift(t):
                    dve.wait_ge(s["an_sd"], t + 1)
                    link(dve.reciprocal(rs[:, t:t + 1], sd[:, t:t + 1]))
                    dve.scalar_tensor_tensor(sh[:, t:t + 1], mv[:, t, 0:1], -1.0, rs[:, t:t + 1], ALU.mult, ALU.mult).then_inc(s["an_shift"], 1)

                dve.wait_ge(s["an_rows"], 64)
                for t in range(TT):
                    c = 0 if t == 0 else 1
                    for h in range(2):
                        sl = slice(h * BANK, (h + 1) * BANK)
                        if w_out is not None:
                            dve.wait_ge(s["an_mm"], 2 * t + h + 1)
                            src = m.bank[(2 * t + h) % 8][:, :]
                        else:
                            src = y[:, t, sl]
                        dve.tensor_tensor(tmp[:, t % 2, sl], src, gate[:, c, sl], ALU.mult).then_inc(s["an_free"], 1)
                    if t >= 1:
                        scale_and_shift(t - 1)
                    dve.wait_ge(s["an_free"], 2 * t + 2)
                    link(dve.scalar_tensor_tensor(m.x[:, t, :], m.x[:, t, :], ALPHA, tmp[:, t % 2, :], ALU.mult, ALU.add))
                    dve.bn_stats(st[:, t, 0, :], m.x[:, t, 0:BANK])
                    link(dve.bn_stats(st[:, t, 1, :], m.x[:, t, BANK:D]))
                    dve.bn_aggr(mv[:, t, :], st[:, t, :, :].rearrange("p a b -> p (a b)")).then_inc(s["an_var"], 1)
                    dve.wait_ge(s["an_var"], t + 1)
                scale_and_shift(TT - 1)


def store_outputs(nc, m):
    with ExitStack() as ctx:
        s = sems(ctx, nc, "so_out")
        with nc.Block() as block:
            @block.sync
            def _(sp):
                sp.dma_start(m.o["y_prompt"], m.x[:, 0, :]).then_inc(s["so_out"], 16)
                sp.dma_start(m.o["y_sample"].rearrange("(t p) d -> p t d", p=P), m.x[:, 1:TT, :]).then_inc(s["so_out"], 16)
                sp.wait_ge(s["so_out"], 32)


PH, NKEY, TOPK = 8, 128, 16
SIDES = 2 * PH
EXPERT_TILES = NKEY
TB = 128
GELU = ACT.Gelu_apprx_tanh
HALF_T = T // 2


def pick(ap, i):
    return ap[:, bass.ds(i, 1)].squeeze(1)


def emit_scores(pe, m, S, s, tokens, last_use):
    for n in range(SIDES + 1):
        if n < SIDES:
            if S.first:
                pe.wait_ge(s[f"ps_w{n % 4}"], 16 * (n // 4 + 1))
            if n >= 2:
                pe.wait_ge(s["ps_qsb"], n - 1)
            for k in range(KD):
                mm = pe.matmul(m.bank[n % 2][:, 0:P], S.wq[:, n, k, :], tokens(k), start=(k == 0), stop=(k == KD - 1))
            mm.then_inc(s["ps_q"], 1)
        if n >= 1:
            u = n - 1
            pe.wait_ge(s["ps_qsb"], u + 1)
            if u == 0:
                last_use()
            mm = pe.matmul(m.bank[4 + u // 4][:, (u % 4) * P:(u % 4 + 1) * P], S.qT[:, u % 2], S.keys[:, u, :], start=True, stop=True)
            mm.then_inc(s["ps_s"], 1)


def emit_q_copies(act, m, S, s):
    for n in range(SIDES):
        act.wait_ge(s["ps_q"], n + 1)
        if n >= 2:
            act.wait_ge(s["ps_s"], n - 1)
        act.activation(S.qT[:, n % 2], m.bank[n % 2][:, 0:P], ACT.Copy).then_inc(s["ps_qsb"], 1)


def peer_first_scores(nc, m, layer, S):
    with ExitStack() as ctx:
        s = sems(ctx, nc, "ps_keys", "ps_w0", "ps_w1", "ps_w2", "ps_w3", "ps_q", "ps_qsb", "ps_s")
        S.first = True
        with nc.Block() as block:
            @block.sync
            def _(sp):
                for n in range(SIDES):
                    if n >= 4:
                        sp.wait_ge(s[f"ps_w{n % 4}"], 16 * (n // 4))
                    sp.dma_start(S.wq[:, n], m.i["peer_wq"][layer, n]).then_inc(s[f"ps_w{n % 4}"], 16)
                    if n == 0:
                        sp.dma_start(S.keys[:, :, :], m.i["peer_k"][layer]).then_inc(s["ps_keys"], 16)

            @block.tensor
            def _(pe):
                pe.wait_ge(s["ps_keys"], 16)
                emit_scores(pe, m, S, s, lambda k: m.hT[:, k, 0:P], lambda: None)

            @block.scalar
            def _(act):
                emit_q_copies(act, m, S, s)
        S.first = False


def top16(dve, wait, rows, work, vals, idx):
    for r, v in zip(rows, vals):
        ins = dve.max(v[:, 0:8], r)
    wait(ins)
    for r, w, v, i in zip(rows, work, vals, idx):
        dve.max_index(i[:, 0:8], v[:, 0:8], r)
        ins = dve.match_replace(w, v[:, 0:8], r, -3.0e38)
    wait(ins)
    for w, v in zip(work, vals):
        ins = dve.max(v[:, 8:16], w)
    wait(ins)
    for w, v, i in zip(work, vals, idx):
        ins = dve.max_index(i[:, 8:16], v[:, 8:16], w)
    wait(ins)


def peer_select(nc, m, S, selT):
    with ExitStack() as ctx:
        sc = buf(ctx, nc, "sc", P, SIDES, NKEY)
        sc2 = buf(ctx, nc, "sc2", P, SIDES, NKEY)
        vals = buf(ctx, nc, "vals", P, SIDES, TOPK)
        idx = buf(ctx, nc, "idx", P, SIDES, TOPK, dtype=U32)
        idxf = buf(ctx, nc, "idxf", P, SIDES, TOPK)
        cand = buf(ctx, nc, "cand", P, PH, TOPK * TOPK)
        cand2 = buf(ctx, nc, "cand2", P, PH, TOPK * TOPK)
        best = buf(ctx, nc, "best", P, PH, TOPK)
        pos = buf(ctx, nc, "pos_u", P, PH, TOPK, dtype=U32)
        place = buf(ctx, nc, "place", P, 2, PH * TOPK, dtype=U32)
        placef = buf(ctx, nc, "placef", P, 2, PH * TOPK)
        eq = buf(ctx, nc, "eq", P, 2, PH * TOPK, TOPK)
        sel = buf(ctx, nc, "sel", P, 3, PH * TOPK)
        gate = buf(ctx, nc, "gatex", P, PH, TOPK)
        norm = buf(ctx, nc, "norm", P, 2, PH)
        iota = m.iota
        s = sems(ctx, nc, "pk_chain", "pk_dif", "pk_exp", "pk_sel", "pk_tr", "pk_out", "pk_sc", "ps_q", "ps_qsb", "ps_s")

        def tile(t, more):
            with nc.Block() as block:
                @block.vector
                def _(dve):
                    link = linker(dve, s["pk_chain"])
                    dve.wait_ge(s["pk_sc"], 4)
                    I = range(SIDES)
                    top16(dve, link, [sc[:, i, :] for i in I], [sc2[:, i, :] for i in I], [vals[:, i, :] for i in I], [idx[:, i, :] for i in I])
                    dve.tensor_copy(idxf[:, :, :], idx[:, :, :])
                    v = vals[:, :, :].rearrange("p (h s) k -> p h s k", s=2)
                    shape = [P, PH, TOPK, TOPK]
                    link(dve.tensor_tensor(cand[:, :, :].rearrange("p h (a b) -> p h a b", a=TOPK), v[:, :, 0, :].unsqueeze(3).broadcast_to(shape),
                                           v[:, :, 1, :].unsqueeze(2).broadcast_to(shape), ALU.add))
                    H = range(PH)
                    top16(dve, link, [cand[:, i, :] for i in H], [cand2[:, i, :] for i in H], [best[:, i, :] for i in H], [pos[:, i, :] for i in H])
                    dve.tensor_tensor(gate[:, :, :], best[:, :, :], best[:, :, 0:1].broadcast_to([P, PH, TOPK]), ALU.subtract).then_inc(s["pk_dif"], 1)
                    pf = pos[:, :, :].rearrange("p h k -> p (h k)")
                    dve.tensor_scalar(place[:, 0, :], pf, 4, None, ALU.logical_shift_right)
                    link(dve.tensor_scalar(place[:, 1, :], pf, TOPK - 1, None, ALU.bitwise_and))
                    link(dve.tensor_copy(placef[:, :, :], place[:, :, :]))
                    for side in range(2):
                        ins = dve.tensor_tensor(eq[:, side], placef[:, side, :].unsqueeze(2).broadcast_to([P, PH * TOPK, TOPK]),
                                                iota[:, 0:TOPK].unsqueeze(1).broadcast_to([P, PH * TOPK, TOPK]), ALU.is_equal)
                    link(ins)
                    iv = idxf[:, :, :].rearrange("p (h s) k -> p h s k", s=2)
                    for side in range(2):
                        e = eq[:, side].rearrange("p (h q) k -> p h q k", h=PH)
                        ins = dve.tensor_tensor(e, e, iv[:, :, side, :].unsqueeze(2).broadcast_to(shape), ALU.mult)
                    link(ins)
                    for side in range(2):
                        ins = dve.tensor_reduce(sel[:, side, :], eq[:, side], mybir.AxisListType.X, ALU.add)
                    dve.wait_ge(s["pk_exp"], 1)
                    link(dve.tensor_reduce(norm[:, 0, :], gate[:, :, :], mybir.AxisListType.X, ALU.add))
                    link(dve.reciprocal(norm[:, 1, :], norm[:, 0, :]))
                    dve.tensor_tensor(sel[:, 2, :].rearrange("p (h k) -> p h k", h=PH), gate[:, :, :],
                                      norm[:, 1, :].unsqueeze(2).broadcast_to([P, PH, TOPK]), ALU.mult).then_inc(s["pk_sel"], 1)

                @block.scalar
                def _(act):
                    for b in range(4):
                        act.activation(sc[:, 4 * b:4 * b + 4, :].rearrange("p a n -> p (a n)"), m.bank[4 + b][:, :], ACT.Copy).then_inc(s["pk_sc"], 1)
                    if more:
                        emit_q_copies(act, m, S, s)
                    act.wait_ge(s["pk_dif"], 1)
                    act.activation(gate[:, :, :], gate[:, :, :], ACT.Exp).then_inc(s["pk_exp"], 1)
                    act.wait_ge(s["pk_tr"], 1)
                    act.activation(selT[:, :, bass.ds(t * P, P)], m.bank[3][:, 0:3 * P].rearrange("p (a t) -> p a t", a=3), ACT.Copy).then_inc(s["pk_out"], 1)
                    act.wait_ge(s["pk_out"], 1)

                @block.tensor
                def _(pe):
                    if more:
                        emit_scores(pe, m, S, s, lambda k: m.hT[:, k, bass.ds(t * P + P, P)], lambda: pe.wait_ge(s["pk_sc"], 4))
                    pe.wait_ge(s["pk_sel"], 1)
                    for a in range(3):
                        mm = pe.transpose(m.bank[3][:, a * P:(a + 1) * P], sel[:, a, :], m.ident[:, :])
                    mm.then_inc(s["pk_tr"], 1)

        with nc.Fori(0, TT - 1) as t:
            tile(t, True)
            clear(nc, s)
        tile(TT - 1, False)


def peer_dense_gates(nc, m, selT):
    QT = 4
    TBLS = 4
    GROUPS = TB // QT
    BLOCKS = T // TB
    with ExitStack() as ctx:
        hot = buf(ctx, nc, "hot", P, TBLS, 2, QT, NKEY)
        G = [buf(ctx, nc, f"gates_sb{i}", P, NKEY, TB) for i in range(2)]
        s = sems(ctx, nc, "pg_hot", "pg_gated", "pg_mm", "pg_sb", "pg_st0", "pg_st1")
        stored = [s["pg_st0"], s["pg_st1"]]
        table = [P, 2, QT, NKEY]
        with nc.Block() as block:
            @block.vector
            def _(dve):
                with dve.Fori(0, BLOCKS * GROUPS // TBLS) as r:
                    for u in range(TBLS):
                        k = TBLS * r + u
                        dve.wait_ge(s["pg_mm"], k + 1)
                        dve.tensor_tensor(hot[:, u], selT[:, 0:2, bass.ds(k * QT, QT)].unsqueeze(3).broadcast_to(table),
                                          m.iota[:, :].unsqueeze(1).unsqueeze(1).broadcast_to(table), ALU.is_equal).then_inc(s["pg_hot"], 1)

            @block.gpsimd
            def _(pool):
                with pool.Fori(0, BLOCKS * GROUPS // TBLS) as r:
                    for u in range(TBLS):
                        k = TBLS * r + u
                        pool.wait_ge(s["pg_hot"], k + 1)
                        pool.tensor_tensor(hot[:, u, 0], hot[:, u, 0], selT[:, 2, bass.ds(k * QT, QT)].unsqueeze(2).broadcast_to([P, QT, NKEY]),
                                           ALU.mult).then_inc(s["pg_gated"], 1)

            @block.tensor
            def _(pe):
                pe.sem_inc(s["pg_mm"], TBLS)
                with pe.Fori(0, BLOCKS * GROUPS // TBLS) as r:
                    for u in range(TBLS):
                        k = TBLS * r + u
                        pe.wait_ge(s["pg_gated"], k + 1)
                        pe.wait_ge(s["pg_sb"], k + 1)
                        for q in range(QT):
                            mm = pe.matmul(m.bank[u][:, q * P:(q + 1) * P], hot[:, u, 1, q, :], hot[:, u, 0, q, :], start=True, stop=True)
                        mm.then_inc(s["pg_mm"], 1)

            @block.scalar
            def _(act):
                act.sem_inc(s["pg_sb"], TBLS)
                for b in range(BLOCKS):
                    if b >= 2:
                        act.wait_ge(stored[b % 2], 16 * (b // 2))
                    with act.Fori(0, GROUPS // TBLS) as r:
                        for u in range(TBLS):
                            act.wait_ge(s["pg_mm"], TBLS * r + (b * GROUPS + u + 1 + TBLS))
                            act.activation(G[b % 2][:, :, bass.ds(r * 16 + 4 * u, 4)].rearrange("p i t -> p t i"),
                                           m.bank[u][:, :].rearrange("p (t i) -> p t i", t=4), ACT.Copy).then_inc(s["pg_sb"], 1)

            @block.sync
            def _(sp):
                for b in range(BLOCKS):
                    sp.wait_ge(s["pg_sb"], (b + 1) * GROUPS + TBLS)
                    sp.dma_start(m.gates[:, :, b * TB:(b + 1) * TB].rearrange("a i t -> i a t"), G[b % 2][:, :, :]).then_inc(stored[b % 2], 16)
                for b in range(BLOCKS - 2, BLOCKS):
                    sp.wait_ge(stored[b % 2], 16 * (b // 2 + 1))


def peer_experts(nc, m, layer, yacc):
    NB = 4
    TURNS = EXPERT_TILES // NB
    PARTS = ((0, 0), (0, 1), (1, 0))
    with ExitStack() as ctx:
        hs = buf(ctx, nc, "h_parts", P, 2, KD, T, dtype=F32R)
        hraw = m.hT[:, :, :].rearrange("p k t -> p (k t)")
        u_in = hraw[:, 0:4 * KD * P].rearrange("p (a k e) -> p a k e", a=4, k=KD)
        us = buf(ctx, nc, "u_parts", P, 2, 2, KD, P, dtype=F32R)
        v_in = buf(ctx, nc, "v_in", P, NB, D)
        vs = buf(ctx, nc, "v_parts", P, NB, 2, D, dtype=F32R)
        g_in = buf(ctx, nc, "g_in", P, 4, T)
        ge = buf(ctx, nc, "ge", P, 2, T)
        gg = buf(ctx, nc, "gg", P, 2, T)
        gs = buf(ctx, nc, "gg_parts", P, NB, 2, T, dtype=F32R)
        s = sems(ctx, nc, "pe_hhi", "pe_h", "pe_s", "pe_gelu", "pe_mul", "pe_uhi", "pe_ulo", "pe_vhi", "pe_vlo", "pe_ghi", "pe_glo", "pe_y", "pe_add", "pe_clear",
                 *[f"pe_u{i}" for i in range(4)], *[f"pe_g{i}" for i in range(4)], *[f"pe_v{i}" for i in range(4)])
        yb = [m.bank[4 + i] for i in range(4)]

        def u_landed(eng, r, j):
            eng.wait_ge(s[f"pe_u{j % 4}"], 16 * r + 16 * (j // 4 + 1))

        with nc.Block() as block:
            @block.sync
            def _(sp):
                sp.wait_ge(s["pe_h"], KD)
                with sp.Fori(0, TURNS) as r:
                    for j in range(NB):
                        e = NB * r + j
                        sp.wait_ge(s["pe_ulo"], e + 1)
                        sp.dma_start(u_in[:, j], m.i["peer_u"][layer, bass.ds(e, 1)].squeeze(0)).then_inc(s[f"pe_u{j}"], 16)
                        sp.wait_ge(s["pe_mul"], e + 1)
                        sp.dma_start(g_in[:, j], m.gates[bass.ds(e, 1)].squeeze(0)).then_inc(s[f"pe_g{j}"], 16)
                        sp.wait_ge(s["pe_vlo"], e + 1)
                        sp.dma_start(v_in[:, j], m.i["peer_v"][layer, bass.ds(e, 1)].squeeze(0)).then_inc(s[f"pe_v{j}"], 16)
                for j in range(2):
                    sp.wait_ge(s["pe_ulo"], EXPERT_TILES + j + 1)
                    sp.dma_start(u_in[:, j], m.i["peer_u"][layer, j]).then_inc(s[f"pe_u{j}"], 16)

            @block.tensor
            def _(pe):
                pe.sem_inc(s["pe_y"], 20)
                pe.wait_ge(s["pe_h"], KD)
                with pe.Fori(0, TURNS) as r:
                    for j in range(NB):
                        e = NB * r + j
                        pe.wait_ge(s["pe_ulo"], e + 5)
                        pe.wait_ge(s["pe_gelu"], e + 1)
                        for k in range(KD):
                            for i, (a, b) in enumerate(PARTS):
                                for c in range(2):
                                    mm = pe.matmul(m.bank[2 * (j % 2) + c][:, 0:HALF_T], us[:, j % 2, a, k, :], hs[:, b, k, c * HALF_T:(c + 1) * HALF_T],
                                                   start=(k == 0 and i == 0), stop=(k == KD - 1 and i == 2))
                        mm.then_inc(s["pe_s"], 1)
                    for half in range(2):
                        pe.wait_ge(s["pe_glo"], NB * r + 2 * half + 4)
                        pe.wait_ge(s["pe_vlo"], NB * r + 2 * half + 6)
                        for n in range(10 * half, 10 * half + 10):
                            t, c = (n % 10) // 2, n % 2
                            pe.wait_ge(s["pe_add"], 20 * r + n + 1)
                            for j in (2 * half, 2 * half + 1):
                                for i, (a, b) in enumerate(PARTS):
                                    mm = pe.matmul(yb[n % 4][:, :], gs[:, j, a, t * P:(t + 1) * P], vs[:, j, b, c * BANK:(c + 1) * BANK],
                                                   start=(j % 2 == 0 and i == 0), stop=(j % 2 == 1 and i == 2))
                            mm.then_inc(s["pe_y"], 1)

            @block.scalar
            def _(act):
                for k in range(KD):
                    ins = act.activation(hs[:, 0, k], m.hT[:, k], ACT.Copy).then_inc(s["pe_hhi"], 1)
                act.sem_inc(s["pe_gelu"], 2)
                for j in range(2):
                    u_landed(act, 0, j)
                    act.activation(us[:, j, 0], u_in[:, j], ACT.Copy).then_inc(s["pe_uhi"], 1)
                with act.Fori(0, TURNS) as r:
                    for j in range(NB):
                        e = NB * r + j
                        act.wait_ge(s["pe_s"], e + 1)
                        act.wait_ge(s["pe_mul"], e + 3)
                        for c in range(2):
                            ins = act.activation(ge[:, j % 2, c * HALF_T:(c + 1) * HALF_T], m.bank[2 * (j % 2) + c][:, 0:HALF_T], GELU)
                        ins.then_inc(s["pe_gelu"], 1)
                        u_landed(act, r, j + 2)
                        act.activation(us[:, j % 2, 0], u_in[:, (j + 2) % 4], ACT.Copy).then_inc(s["pe_uhi"], 1)
                        act.wait_ge(s[f"pe_v{j}"], 16 * r + 16)
                        act.wait_ge(s["pe_y"], 20 * r + 10 * (j // 2) + 10)
                        act.activation(vs[:, j, 0], v_in[:, j], ACT.Copy).then_inc(s["pe_vhi"], 1)
                        act.wait_ge(s["pe_mul"], e + 5)
                        act.activation(gs[:, j, 0], gg[:, j % 2], ACT.Copy).then_inc(s["pe_ghi"], 1)

            @block.vector
            def _(dve):
                dve.sem_inc(s["pe_ulo"], 4)
                dve.sem_inc(s["pe_mul"], 4)
                dve.sem_inc(s["pe_vlo"], 4)
                dve.sem_inc(s["pe_glo"], 2)
                dve.sem_inc(s["pe_add"], 4)
                dve.memset(yacc[:, :, :], 0.0).then_inc(s["pe_clear"], 1)
                for k in range(KD):
                    dve.wait_ge(s["pe_hhi"], k + 1)
                    dve.tensor_tensor(hs[:, 1, k], m.hT[:, k], hs[:, 0, k].bitcast(F32), ALU.subtract).then_inc(s["pe_h"], 1)

                def u_low(slot, raw, n):
                    dve.wait_ge(s["pe_uhi"], n)
                    dve.tensor_tensor(us[:, slot, 1], u_in[:, raw], us[:, slot, 0].bitcast(F32), ALU.subtract).then_inc(s["pe_ulo"], 1)

                for j in range(2):
                    u_low(j, j, j + 1)
                dve.wait_ge(s["pe_clear"], 1)
                with dve.Fori(0, TURNS) as r:
                    for j in range(NB):
                        e = NB * r + j
                        dve.wait_ge(s["pe_gelu"], e + 3)
                        dve.wait_ge(s[f"pe_g{j}"], 16 * r + 16)
                        dve.wait_ge(s["pe_glo"], e + 1)
                        dve.tensor_tensor(gg[:, j % 2], ge[:, j % 2], g_in[:, j], ALU.mult).then_inc(s["pe_mul"], 1)
                        u_low(j % 2, (j + 2) % 4, e + 3)
                        dve.wait_ge(s["pe_vhi"], e + 1)
                        dve.tensor_tensor(vs[:, j, 1], v_in[:, j], vs[:, j, 0].bitcast(F32), ALU.subtract).then_inc(s["pe_vlo"], 1)
                        dve.wait_ge(s["pe_ghi"], e + 1)
                        dve.tensor_tensor(gs[:, j, 1], gg[:, j % 2], gs[:, j, 0].bitcast(F32), ALU.subtract).then_inc(s["pe_glo"], 1)
                    for n in range(20):
                        y = yacc[:, (n % 10) // 2, (n % 2) * BANK:(n % 2 + 1) * BANK]
                        dve.wait_ge(s["pe_y"], 20 * r + n + 21)
                        dve.tensor_tensor(y, y, yb[n % 4][:, :], ALU.add).then_inc(s["pe_add"], 1)


def peer(nc, m, layer):
    norm_modulate(nc, m, layer, 1)
    with ExitStack() as ctx:
        selT = buf(ctx, nc, "selT", P, 3, T)
        with ExitStack() as inner:
            S = Shared()
            S.wq = buf(inner, nc, "wq", P, SIDES, KD, P)
            S.keys = buf(inner, nc, "keys", P, SIDES, NKEY)
            S.qT = buf(inner, nc, "qT", P, 2, P)
            peer_first_scores(nc, m, layer, S)
            peer_select(nc, m, S, selT)
        peer_dense_gates(nc, m, selT)
    with ExitStack() as ctx:
        yacc = buf(ctx, nc, "yacc", P, TT, D)
        peer_experts(nc, m, layer, yacc)
        add_and_norm(nc, m, layer, 1, y=yacc)


LM_RING = 4
UNITS = (LEVELS - 1) * TT


def project_shifted(pe, m, w, q, mm_sem, first=0):
    for c, a, n in SEGS:
        for k in range(KD):
            mm = pe.matmul(m.bank[first + 2 * q + 1 - c][:, 0:n], w[:, q, k, :], m.hT[:, k, a:a + n], start=(k == 0), stop=(k == KD - 1))
    mm.then_inc(mm_sem, 1)


def to_padded(act, m, zp, q, sem, first=0):
    for c, _, n in SEGS:
        ins = act.activation(zp[:, q, ZOFF[c]:ZOFF[c] + n], m.bank[first + 2 * q + 1 - c][:, 0:n], ACT.Copy)
    ins.then_inc(sem, 1)


def shift_mix(dve, link, zp, tmp, out, mu, omu, hmu):
    link(dve.tensor_tensor(tmp[:, 0:ZW - 2], zp[:, 0:ZW - 2], zp[:, 2:ZW], ALU.add))
    link(dve.tensor_scalar(tmp[:, 0:ZW - 2], tmp[:, 0:ZW - 2], hmu, None, ALU.mult))
    for c, a, n in SEGS:
        z = ZOFF[c]
        ins = dve.scalar_tensor_tensor(out[:, a:a + n], zp[:, z:z + n], omu, tmp[:, z - 1:z - 1 + n], ALU.mult, ALU.add)
        if c == 0:
            link(ins)
    return ins


def lora_and_fourier_inputs(nc, m, L):
    with ExitStack() as ctx:
        w = buf(ctx, nc, "w_rest", P, 5, KD, P)
        zp = buf(ctx, nc, "zp_rest", P, 3, ZW)
        tmp = buf(ctx, nc, "tmp_rest", P, ZW)
        mu = buf(ctx, nc, "mu_rest", P, 3, 3)
        s = sems(ctx, nc, "lf_w", "lf_mu", "lf_mm", "lf_zp", "lf_zero", "lf_chain", "lf_mix", "lf_fn", "lf_act")
        with nc.Block() as block:
            @block.sync
            def _(sp):
                sp.dma_start(w[:, :, :, :], m.i["w_rest"]).then_inc(s["lf_w"], 16)
                sp.dma_start(mu[:, 0, :], m.i["mu_rest"]).then_inc(s["lf_mu"], 16)

            @block.gpsimd
            def _(pool):
                pool.memset(zp[:, :, :], 0.0).then_inc(s["lf_zero"], 1)

            @block.tensor
            def _(pe):
                pe.wait_ge(s["lf_w"], 16)
                for q in range(3):
                    project_shifted(pe, m, w, q, s["lf_mm"])
                pe.wait_ge(s["lf_zp"], 2)
                for q in (3, 4):
                    for c, a, n in SEGS:
                        for k in range(KD):
                            mm = pe.matmul(m.bank[2 * (q - 3) + 1 - c][:, 0:n], w[:, q, k, :], m.hT[:, k, a:a + n], start=(k == 0), stop=(k == KD - 1))
                    mm.then_inc(s["lf_mm"], 1)

            @block.scalar
            def _(act):
                act.wait_ge(s["lf_zero"], 1)
                for q in range(3):
                    act.wait_ge(s["lf_mm"], q + 1)
                    to_padded(act, m, zp, q, s["lf_zp"])
                for q in range(2):
                    act.wait_ge(s["lf_mm"], q + 4)
                    for c, a, n in SEGS:
                        ins = act.activation(L.zf[:, q, a:a + n], m.bank[2 * q + 1 - c][:, 0:n], ACT.Copy)
                ins.then_inc(s["lf_fn"], 1)
                act.wait_ge(s["lf_mix"], 3)
                act.activation(L.zw[:, :], L.zw[:, :], ACT.Tanh)
                act.activation(L.zg[:, :], L.zg[:, :], ACT.Sigmoid).then_inc(s["lf_act"], 1)
                act.wait_ge(s["lf_act"], 1)

            @block.vector
            def _(dve):
                link = linker(dve, s["lf_chain"])
                dve.wait_ge(s["lf_mu"], 16)
                dve.tensor_scalar(mu[:, 1, :], mu[:, 0, :], -1.0, 1.0, ALU.mult, ALU.add)
                link(dve.tensor_scalar(mu[:, 2, :], mu[:, 0, :], 0.5, None, ALU.mult))
                for q, out in enumerate((L.zw, L.za, L.zg)):
                    dve.wait_ge(s["lf_zp"], q + 1)
                    shift_mix(dve, link, zp[:, q, :], tmp, out, None, mu[:, 1, q:q + 1], mu[:, 2, q:q + 1]).then_inc(s["lf_mix"], 1)
                    dve.wait_ge(s["lf_mix"], q + 1)


def rwkv_pairs(nc, m, L):
    with ExitStack() as ctx:
        region = buf(ctx, nc, "region", P, max(4 * ZW + 12 * T, (4 * TT + LM_RING) * 4 * P))
        taken = [0]

        def part(*shape):
            n = int(np.prod(shape))
            at = region[:, taken[0]:taken[0] + n]
            taken[0] += n
            names = "abcd"[:len(shape)]
            return at.rearrange(f"p ({' '.join(names)}) -> p {' '.join(names)}", **dict(zip(names, shape)))

        w = buf(ctx, nc, "w_rkv", P, 3, KD, P)
        zp = part(3, ZW)
        tmp = part(ZW)
        sw, sa, kd, cum, exc, inc = (part(2, T) for _ in range(6))
        taken[0] = 0
        G = part(TT, 4, 4 * P)
        LM = part(LM_RING, 4, P)
        lw = buf(ctx, nc, "lora_w", P, 3, P)
        pc = buf(ctx, nc, "pcol", P, NPC)
        pd = buf(ctx, nc, "pder", P, 8)
        rkv = buf(ctx, nc, "rkv", P, 3, T)
        kk = buf(ctx, nc, "kk", P, T)
        nrm = buf(ctx, nc, "nrm", P, T)
        gT = buf(ctx, nc, "gT", P, T)
        wend = buf(ctx, nc, "wend", P, 2, T // CH)
        xs = m.x[:, :, :].rearrange("p a b -> p (a b)")
        half = TT * D // 2
        AR = xs[:, 0:half].rearrange("p (d t j n) -> p d t j n", d=2, t=TT, j=2)
        BKt = xs[:, half:2 * half].rearrange("p (d j t n) -> p d j t n", d=2, j=2, t=TT)
        BK = buf(ctx, nc, "BK", P, 2, 2, T)
        vt = buf(ctx, nc, "vt", P, TT, P)
        Y = BK[:, 0].rearrange("p j (t n) -> p j t n", n=P)
        vm = BK[:, 1].rearrange("p h (t n) -> p t h n", n=P)
        bonus = buf(ctx, nc, "bonus", P, T)
        XT = buf(ctx, nc, "XT", P, TT, 4, P)
        X = buf(ctx, nc, "X", P, TT, 4, P)
        T1 = buf(ctx, nc, "T1", P, 3, 4, P)
        tm = buf(ctx, nc, "tm", P, 2, 4, P)
        st = buf(ctx, nc, "state", P, 2, 2, P)
        Zs = T1[:, 0].rearrange("p (a b) n -> p a b n", a=2)
        Um = T1[:, 1].rearrange("p (a b) n -> p a b n", a=2)
        sup = T1[:, 2, 0:2]
        stat = buf(ctx, nc, "stat", P, 4, TT * 2)
        gm = buf(ctx, nc, "gmask", P, 2, 4 * P)
        lm = buf(ctx, nc, "lmask", P, LEVELS, 2, P)
        four = [P, 4, P]
        i4 = m.ident[:, :].unsqueeze(1).broadcast_to(four)
        reset = buf(ctx, nc, "reset", P, T)
        bd = buf(ctx, nc, "bd", P, P)
        hm = buf(ctx, nc, "hm", P, 4)
        Z_BANK = 2
        tab = sems(ctx, nc, "rt_tables", "rt_away", "rt_back", "rt_w", "rt_z")
        with nc.Block() as block:
            @block.sync
            def _(sp):
                for dst, src in ((gm, m.i["gmask"]), (lm, m.i["lmask"]), (reset, m.i["reset"]), (bd, m.i["bd"]), (hm, m.i["hm"])):
                    sp.dma_start(dst[:], src).then_inc(tab["rt_tables"], 16)
                sp.dma_start(m.tokens, m.x[:, :, :]).then_inc(tab["rt_away"], 16)
                sp.dma_start(w[:, :], m.i["w_rkv"][0]).then_inc(tab["rt_w"], 16)
                sp.wait_ge(tab["rt_tables"], 5 * 16)
                sp.wait_ge(tab["rt_away"], 16)

            @block.tensor
            def _(pe):
                pe.wait_ge(tab["rt_w"], 16)
                for q in range(3):
                    project_shifted(pe, m, w, q, tab["rt_z"], Z_BANK)
                pe.wait_ge(tab["rt_z"], 3)

        s = sems(ctx, nc, "rk_w", "rk_zero", "rk_par", "rk_state", "rk_z", "rk_zp", "rk_chain", "rk_sq", "rk_ss", "rk_sqrt", "rk_lora", "rk_sig",
                 "rk_g", "rk_gsb", "rk_vt", "rk_vtsb", "rk_bsum", "rk_kd", "rk_r", "rk_bmm", "rk_cum", "rk_exp", "rk_ab", "rk_bk", "rk_bksb", "rk_v",
                 "rk_gmm", "rk_gsb2", "rk_lt", "rk_x", "rk_xt", "rk_lm", "rk_t1", "rk_t1sb", "rk_t2t", "rk_xtr", "rk_xsb", "rk_rs", "rk_zmm", "rk_zsb", "rk_umm", "rk_usb", "rk_ymm", "rk_ysb",
                 "rk_smm", "rk_s", "rk_s0", "rk_gn", "rk_gnsd", "rk_yn", "rk_ytr", "rk_yact", "rk_out", "rk_store", "rk_vm", "rk_actc")
        STEPS = [(1, 0), (0, 0), (1, 1), (0, 1)] + [(1, c) for c in range(2, 8)]
        TABLE_ORDER = (1, 2, 3, 0)
        NCHUNK = [T_CTX // CH, T_LAT // CH]

        def place(g, c, d):
            cc = c if d == 0 else NCHUNK[g] - 1 - c
            return (0 if g == 0 else 1) + cc // 2, cc % 2, (0 if g == 0 else NCHUNK[0]) + cc

        def turn(f, more):
            with nc.Block() as block:
                @block.sync
                def _(sp):
                    sp.dma_start(pc[:, :], m.i["pcol"][bass.ds(f, 1)].squeeze(0)).then_inc(s["rk_par"], 16)
                    sp.dma_start(lw[:, :, :], m.i["lora_w"][bass.ds(f, 1)].squeeze(0)).then_inc(s["rk_par"], 16)
                    sp.wait_ge(s["rk_s0"], 1)
                    for d in range(2):
                        for h in range(2):
                            sp.dma_start(st[CH * h:CH * h + CH, 1, d, CH * h:CH * h + CH], m.i["state"][bass.ds(f, 1), d, h].squeeze(0)).then_inc(s["rk_state"], 16)
                    if more:
                        sp.dma_start(w[:, :], m.i["w_rkv"][bass.ds(f + 1, 1)].squeeze(0)).then_inc(s["rk_w"], 16)
                    sp.wait_ge(s["rk_s"], 2 * len(STEPS))
                    for d in range(2):
                        for h in range(2):
                            sp.dma_start(m.o["states"][bass.ds(f, 1), d, h].squeeze(0), st[CH * h:CH * h + CH, 0, d, CH * h:CH * h + CH]).then_inc(s["rk_store"], 16)
                    sp.wait_ge(s["rk_store"], 64)

                @block.gpsimd
                def _(pool):
                    pool.memset(zp, 0.0).then_inc(s["rk_zero"], 1)
                    pool.memset(st[:, :, :, :], 0.0).then_inc(s["rk_s0"], 1)
                    pool.wait_ge(s["rk_sig"], 4)
                    pool.wait_ge(s["rk_r"], 1)
                    for d in range(2):
                        pool.tensor_scalar(kd[:, d], sa[:, d], pc[:, PC_KA:PC_KA + 1], pd[:, 6:7], ALU.mult, ALU.add).then_inc(s["rk_kd"], 1)
                        pool.wait_ge(s["rk_kd"], 2 * d + 1)
                        pool.tensor_tensor(kd[:, d], kd[:, d], rkv[:, 1, :], ALU.mult).then_inc(s["rk_kd"], 1)
                    pool.wait_ge(s["rk_kd"], 4)
                    pool.tensor_tensor(bonus[:, :], kd[:, 0], kd[:, 1], ALU.add).then_inc(s["rk_kd"], 1)
                    pool.wait_ge(s["rk_kd"], 5)
                    pool.tensor_tensor(bonus[:, :], bonus[:, :], rkv[:, 0, :], ALU.mult).then_inc(s["rk_kd"], 1)
                    pool.wait_ge(s["rk_kd"], 6)
                    pool.tensor_scalar(bonus[:, :], bonus[:, :], pd[:, 7:8], None, ALU.mult).then_inc(s["rk_bsum"], 1)
                    for n in range(UNITS):
                        lv, t = 1 + n // TT, n % TT
                        if lv == 1:
                            pool.wait_ge(s["rk_gsb2"], 4 * t + 4)
                        if n >= LM_RING:
                            pool.wait_ge(s["rk_t1"], n - LM_RING + 1)
                        for d in range(2):
                            ins = pool.tensor_tensor(LM[:, n % LM_RING, 2 * d:2 * d + 2], G[:, t, 2 * d:2 * d + 2, 0:P],
                                                     lm[:, lv, d].unsqueeze(1).broadcast_to([P, 2, P]), ALU.mult)
                        ins.then_inc(s["rk_lm"], 1)
                    pool.wait_ge(s["rk_gmm"], 4 * TT)
                    for t in range(TT):
                        for h in range(2):
                            ins = pool.tensor_scalar(vm[:, t, h, :], vt[:, t, :], hm[:, h:h + 1], None, ALU.mult)
                    ins.then_inc(s["rk_vm"], 1)

                @block.tensor
                def _(pe):
                    pe.wait_ge(s["rk_par"], 32)
                    pe.wait_ge(s["rk_zp"], 3)
                    for b, (z, j, d) in enumerate(((L.zw, 0, 0), (L.zw, 0, 1), (L.za, 1, 0), (L.za, 1, 1))):
                        r = slice(64 * d, 64 * d + 64)
                        for c, a, n in SEGS:
                            mm = pe.matmul(m.bank[2 * b + 1 - c][:, 0:n], lw[r, j, :], z[r, a:a + n], start=True, stop=True)
                        mm.then_inc(s["rk_lora"], 1)
                    pe.wait_ge(s["rk_sig"], 1)
                    pe.wait_ge(s["rk_sq"], 1)
                    for c, a, n in SEGS:
                        mm = pe.matmul(m.bank[1 - c][:, 0:n], bd[:, :], nrm[:, a:a + n], start=True, stop=True)
                    mm.then_inc(s["rk_ss"], 1)
                    pe.wait_ge(s["rk_sig"], 2)
                    for c, a, n in SEGS:
                        mm = pe.matmul(m.bank[3 - c][:, 0:n], lw[:, 2, :], L.zg[:, a:a + n], start=True, stop=True)
                    mm.then_inc(s["rk_g"], 1)
                    pe.wait_ge(s["rk_sig"], 4)
                    pe.wait_ge(s["rk_v"], 1)
                    for t in range(TT):
                        mm = pe.transpose(m.bank[6 + t // 4][:, (t % 4) * P:(t % 4 + 1) * P], rkv[:, 2, t * P:(t + 1) * P], m.ident[:, :])
                    mm.then_inc(s["rk_vt"], 1)
                    pe.wait_ge(s["rk_bsum"], 1)
                    for c, a, n in SEGS:
                        mm = pe.matmul(m.bank[5 - c][:, 0:n], bd[:, :], bonus[:, a:a + n], start=True, stop=True)
                    mm.then_inc(s["rk_bmm"], 1)
                    pe.wait_ge(s["rk_gsb"], 1)
                    pe.wait_ge(s["rk_sqrt"], 1)
                    for d in range(2):
                        pe.wait_ge(s["rk_bk"], d + 1)
                        if d == 1:
                            pe.wait_ge(s["rk_yact"], 1)
                            pe.wait_ge(s["rk_vtsb"], 2)
                        for j in range(2):
                            for t in range(TT):
                                mm = pe.transpose(m.bank[4 * d + 2 * j + t // 4][:, (t % 4) * P:(t % 4 + 1) * P], BK[:, d, j, t * P:(t + 1) * P], m.ident[:, :])
                            mm.then_inc(s["rk_x"], 1)
                    pe.wait_ge(s["rk_bksb"], 4)

                    def tables(t):
                        for dh in TABLE_ORDER:
                            d, h = dh // 2, dh % 2
                            if t >= 2 and dh == 0:
                                pe.wait_ge(s["rk_xt"], t - 1)
                            r = slice(64 * h, 64 * h + 64)
                            for j in range(2):
                                mm = pe.matmul(m.bank[4 * (t % 2) + dh][:, j * 256:(j + 1) * 256], BK[r, d, j, t * P:(t + 1) * P],
                                               AR[r, d, t].rearrange("p a t -> p (a t)"), start=True, stop=True)
                            mm.then_inc(s["rk_gmm"], 1)

                    tables(0)
                    for t in range(TT):
                        if t + 1 < TT:
                            tables(t + 1)
                        pe.wait_ge(s["rk_gsb2"], 4 * t + 4)
                        for dh in range(4):
                            mm = pe.transpose(m.bank[4 * (t % 2)][:, dh * P:(dh + 1) * P], G[:, t, dh, 0:P], m.ident[:, :])
                        mm.then_inc(s["rk_lt"], 1)
                    for n in range(UNITS + 2):
                        if n < UNITS:
                            t = n % TT
                            pe.wait_ge(s["rk_lm"], n + 1)
                            if n < TT:
                                pe.wait_ge(s["rk_xt"], TT)
                            else:
                                pe.wait_ge(s["rk_xsb"], n - TT + 1)
                            if n >= 2:
                                pe.wait_ge(s["rk_t1sb"], n - 1)
                            for dh in range(4):
                                mm = pe.matmul(m.bank[5 + n % 2][:, dh * P:(dh + 1) * P], LM[:, n % LM_RING, dh], X[:, t, dh], start=True, stop=True)
                            mm.then_inc(s["rk_t1"], 1)
                        if 1 <= n <= UNITS:
                            u = n - 1
                            pe.wait_ge(s["rk_t1sb"], u + 1)
                            if u >= 2:
                                pe.wait_ge(s["rk_xt"], TT + u - 1)
                            for dh in range(4):
                                mm = pe.matmul(m.bank[(7, 0)[u % 2]][:, dh * P:(dh + 1) * P], T1[:, u % 3, dh], XT[:, u % TT, dh], start=True, stop=True)
                            mm.then_inc(s["rk_t2t"], 1)
                        if n >= 2 and n - 2 < UNITS - TT:
                            u = n - 2
                            pe.wait_ge(s["rk_xt"], TT + u + 1)
                            if u >= 2:
                                pe.wait_ge(s["rk_xsb"], u - 1)
                            for dh in range(4):
                                mm = pe.transpose(m.bank[1 + u % 2][:, dh * P:(dh + 1) * P], XT[:, u % TT, dh], m.ident[:, :])
                            mm.then_inc(s["rk_xtr"], 1)
                    pe.wait_ge(s["rk_xt"], TT + UNITS)
                    pe.wait_ge(s["rk_vm"], 1)
                    pe.wait_ge(s["rk_state"], 64)
                    for n, (g, c) in enumerate(STEPS):
                        if c > 0:
                            before = max(i for i in range(n) if STEPS[i][0] == g)
                            pe.wait_ge(s["rk_s"], 2 * before + 2)
                        if n >= 2:
                            pe.wait_ge(s["rk_zsb"], n - 1)
                        zb, ub, sb, ob = (m.bank[2 * b + n % 2] for b in range(4))
                        for d in range(2):
                            t, half, _ = place(g, c, d)
                            pe.matmul(zb[:, d * P:(d + 1) * P], AR[:, d, t, 0], st[:, g, d], start=(d == 0), stop=False, skip_group_check=True)
                            for h in range(2):
                                mm = pe.matmul(zb[:, d * P + 64 * h:d * P + 64 * h + 64], G[:, t, 2 * d + h, 2 * P:3 * P], vt[:, t, 64 * h:64 * h + 64],
                                               start=False, stop=True, skip_group_check=True)
                        mm.then_inc(s["rk_zmm"], 1)
                        if n >= 2:
                            pe.wait_ge(s["rk_ysb"], 2 * n - 2)
                        for d in range(2):
                            t, half, _ = place(g, c, d)
                            pe.matmul(ob[:, d * P:(d + 1) * P], AR[:, d, t, 1], st[:, g, d], start=(d == 0), stop=False, skip_group_check=True)
                            for h in range(2):
                                mm = pe.matmul(ob[:, d * P + 64 * h:d * P + 64 * h + 64], G[:, t, 2 * d + h, 3 * P:4 * P], vt[:, t, 64 * h:64 * h + 64],
                                               start=False, stop=False, skip_group_check=True)
                        mm.then_inc(s["rk_rs"], 1)
                        pe.wait_ge(s["rk_zsb"], n + 1)
                        if n >= 2:
                            pe.wait_ge(s["rk_usb"], 2 * n - 2)
                        for d in range(2):
                            t, half, _ = place(g, c, d)
                            for h in range(2):
                                mm = pe.matmul(ub[:, d * P + 64 * h:d * P + 64 * h + 64], XT[:, t, 2 * d + h], Zs[:, n % 2, d, 64 * h:64 * h + 64], start=True, stop=True)
                        mm.then_inc(s["rk_umm"], 1)
                        if n >= 2:
                            pe.wait_ge(s["rk_s"], 2 * n - 2)
                        for d in range(2):
                            t, half, _ = place(g, c, d)
                            pe.matmul(sb[:, d * P:(d + 1) * P], BKt[:, d, 1, t], vm[:, t, half], start=(d == 0), stop=False, skip_group_check=True)
                        pe.wait_ge(s["rk_usb"], 2 * n + 2)
                        for d in range(2):
                            t, half, _ = place(g, c, d)
                            mm = pe.matmul(sb[:, d * P:(d + 1) * P], BKt[:, d, 0, t], Um[:, n % 2, d], start=False, stop=True, skip_group_check=True)
                        mm.then_inc(s["rk_smm"], 1)
                        for d in range(2):
                            t, half, _ = place(g, c, d)
                            for h in range(2):
                                mm = pe.matmul(ob[:, d * P + 64 * h:d * P + 64 * h + 64], G[:, t, 2 * d + h, P:2 * P], Um[:, n % 2, d, 64 * h:64 * h + 64],
                                               start=False, stop=True, skip_group_check=True)
                        mm.then_inc(s["rk_ymm"], 1)
                    if more:
                        pe.wait_ge(s["rk_w"], 16)
                        project_shifted(pe, m, w, 0, s["rk_z"], Z_BANK)
                    pe.wait_ge(s["rk_yn"], 1)
                    for t in range(TT):
                        mm = pe.transpose(m.bank[t // 4][:, (t % 4) * P:(t % 4 + 1) * P], Y[:, 0, t, :], m.ident[:, :])
                    mm.then_inc(s["rk_ytr"], 1)
                    if more:
                        pe.wait_ge(s["rk_s"], 2 * len(STEPS))
                        project_shifted(pe, m, w, 1, s["rk_z"], Z_BANK)
                        pe.wait_ge(s["rk_ysb"], 2 * len(STEPS))
                        project_shifted(pe, m, w, 2, s["rk_z"], Z_BANK)
                        pe.wait_ge(s["rk_z"], 3)

                @block.scalar
                def _(act):
                    act.wait_ge(s["rk_zero"], 1)
                    for q in range(3):
                        to_padded(act, m, zp, q, s["rk_zp"], Z_BANK)
                    for b, (dst, col) in enumerate(((sw[:, 0], PC_W0), (sw[:, 1], PC_W0B), (sa[:, 0], PC_A0), (sa[:, 1], PC_A0B))):
                        act.wait_ge(s["rk_lora"], b + 1)
                        for c, a, n in SEGS:
                            ins = act.activation(dst[:, a:a + n], m.bank[2 * b + 1 - c][:, 0:n], ACT.Sigmoid, bias=pc[:, col:col + 1])
                        ins.then_inc(s["rk_sig"], 1)
                    act.wait_ge(s["rk_ss"], 1)
                    for c, a, n in SEGS:
                        ins = act.activation(nrm[:, a:a + n], m.bank[1 - c][:, 0:n], ACT.Sqrt, bias=m.eps[:, 2:3])
                    ins.then_inc(s["rk_sqrt"], 1)
                    act.wait_ge(s["rk_g"], 1)
                    for c, a, n in SEGS:
                        ins = act.activation(gT[:, a:a + n], m.bank[3 - c][:, 0:n], ACT.Copy)
                    ins.then_inc(s["rk_gsb"], 1)
                    act.wait_ge(s["rk_vt"], 1)
                    act.activation(vt[:, 0:4].rearrange("p a b -> p (a b)"), m.bank[6][:, :], ACT.Copy).then_inc(s["rk_vtsb"], 1)
                    act.activation(vt[:, 4], m.bank[7][:, 0:P], ACT.Copy).then_inc(s["rk_vtsb"], 1)
                    for d in range(2):
                        act.wait_ge(s["rk_cum"], d + 1)
                        act.activation(wend[:, d, :], cum[:, d].rearrange("p (c t) -> p c t", t=CH)[:, :, CH - 1], ACT.Exp, scale=-DECAY_C).then_inc(s["rk_actc"], 1)
                        act.wait_ge(s["rk_actc"], 2 * d + 1)
                        act.activation(cum[:, d], inc[:, d], ACT.Exp, scale=DECAY_C).then_inc(s["rk_actc"], 1)
                        act.activation(exc[:, d], exc[:, d], ACT.Exp, scale=-DECAY_C)
                        act.wait_ge(s["rk_actc"], 2 * d + 2)
                        act.activation(inc[:, d], inc[:, d], ACT.Exp, scale=-DECAY_C).then_inc(s["rk_exp"], 1)
                        if d == 0:
                            act.wait_ge(s["rk_bmm"], 1)
                            for c, a, n in SEGS:
                                ins = act.activation(bonus[:, a:a + n], m.bank[5 - c][:, 0:n], ACT.Copy)
                            ins.then_inc(s["rk_yact"], 1)
                    for n in range(4):
                        act.wait_ge(s["rk_x"], n + 1)
                        d, j = n // 2, n % 2
                        act.activation(BKt[:, d, j, 0:4].rearrange("p a b -> p (a b)"), m.bank[2 * n][:, :], ACT.Copy)
                        act.activation(BKt[:, d, j, 4], m.bank[2 * n + 1][:, 0:P], ACT.Copy).then_inc(s["rk_bksb"], 1)
                    for n in range(UNITS + 2):
                        if n < UNITS:
                            act.wait_ge(s["rk_t1"], n + 1)
                            if n >= 3:
                                act.wait_ge(s["rk_t2t"], n - 2)
                            act.activation(T1[:, n % 3].rearrange("p a b -> p (a b)"), m.bank[5 + n % 2][:, :], ACT.Copy).then_inc(s["rk_t1sb"], 1)
                        if n >= 2 and n - 2 < UNITS - TT:
                            u = n - 2
                            act.wait_ge(s["rk_xtr"], u + 1)
                            act.activation(X[:, u % TT].rearrange("p a b -> p (a b)"), m.bank[1 + u % 2][:, :], ACT.Copy).then_inc(s["rk_xsb"], 1)
                    for n, (g, c) in enumerate(STEPS):
                        act.wait_ge(s["rk_zmm"], n + 1)
                        if n >= 2:
                            act.wait_ge(s["rk_umm"], n - 1)
                        act.activation(Zs[:, n % 2].rearrange("p a b -> p (a b)"), m.bank[n % 2][:, 0:2 * P], ACT.Copy).then_inc(s["rk_zsb"], 1)
                        act.wait_ge(s["rk_ymm"], n + 1)
                        for d in range(2):
                            t, half, _ = place(g, c, d)
                            r = slice(64 * half, 64 * half + 64)
                            act.activation(Y[r, d, t], m.bank[6 + n % 2][r, d * P:(d + 1) * P], ACT.Copy).then_inc(s["rk_ysb"], 1)
                    act.wait_ge(s["rk_gn"], 1)
                    act.activation(stat[:, 2], stat[:, 1], ACT.Sqrt, bias=m.eps[:, 1:2], scale=1.0 / HS).then_inc(s["rk_gnsd"], 1)
                    act.wait_ge(s["rk_ytr"], 1)
                    act.activation(kk[:, 0:4 * P], m.bank[0][:, :], ACT.Identity, scale=pc[:, PC_GNG:PC_GNG + 1], bias=pc[:, PC_GNB:PC_GNB + 1])
                    act.activation(kk[:, 4 * P:T], m.bank[1][:, 0:P], ACT.Identity, scale=pc[:, PC_GNG:PC_GNG + 1], bias=pc[:, PC_GNB:PC_GNB + 1]).then_inc(s["rk_yact"], 1)

                @block.vector
                def _(dve):
                    link = linker(dve, s["rk_chain"])
                    dve.wait_ge(s["rk_par"], 32)
                    dve.tensor_scalar(pd[:, 0:3], pc[:, 0:3], -1.0, 1.0, ALU.mult, ALU.add)
                    dve.tensor_scalar(pd[:, 3:6], pc[:, 0:3], 0.5, None, ALU.mult)
                    dve.tensor_scalar(pd[:, 6:7], pc[:, PC_KA:PC_KA + 1], -1.0, 1.0, ALU.mult, ALU.add)
                    link(dve.tensor_scalar(pd[:, 7:8], pc[:, PC_RK:PC_RK + 1], 0.5, None, ALU.mult))
                    for q in (1, 2, 0):
                        dve.wait_ge(s["rk_zp"], q + 1)
                        ins = shift_mix(dve, link, zp[:, q, :], tmp, rkv[:, q, :], None, pd[:, q:q + 1], pd[:, 3 + q:4 + q])
                        if q == 2:
                            ins.then_inc(s["rk_v"], 1)
                            dve.wait_ge(s["rk_v"], 1)
                        elif q == 0:
                            ins.then_inc(s["rk_r"], 1)
                            dve.wait_ge(s["rk_r"], 1)
                        else:
                            link(ins)
                        if q == 1:
                            link(dve.tensor_scalar(kk[:, :], rkv[:, 1, :], pc[:, PC_KK:PC_KK + 1], None, ALU.mult))
                            dve.tensor_tensor(nrm[:, :], kk[:, :], kk[:, :], ALU.mult).then_inc(s["rk_sq"], 1)
                    r, k, v = rkv[:, 0, :], rkv[:, 1, :], rkv[:, 2, :]
                    for d in range(2):
                        dve.wait_ge(s["rk_sig"], d + 1)
                        link(dve.tensor_tensor_scan(cum[:, d], reset[:, :], sw[:, d], 0.0, ALU.mult, ALU.add))
                        if d == 0:
                            dve.tensor_copy(inc[:, 0], cum[:, 0])
                            dve.tensor_tensor(exc[:, 0], cum[:, 0], sw[:, 0], ALU.subtract).then_inc(s["rk_cum"], 1)
                        else:
                            c3 = cum[:, 1].rearrange("p (c t) -> p c t", t=CH)
                            link(dve.tensor_tensor(exc[:, 1].rearrange("p (c t) -> p c t", t=CH), c3[:, :, CH - 1:CH].broadcast_to([P, T // CH, CH]), c3, ALU.subtract))
                            dve.tensor_tensor(inc[:, 1], exc[:, 1], sw[:, 1], ALU.add).then_inc(s["rk_cum"], 1)
                    dve.wait_ge(s["rk_sqrt"], 1)
                    link(dve.reciprocal(nrm[:, :], nrm[:, :]))
                    link(dve.tensor_tensor(kk[:, :], kk[:, :], nrm[:, :], ALU.mult))
                    for d in range(2):
                        if d == 0:
                            dve.wait_ge(s["rk_sig"], 4)
                            dve.wait_ge(s["rk_kd"], 4)
                        link(dve.tensor_tensor(sa[:, d], sa[:, d], kk[:, :], ALU.mult))
                        dve.wait_ge(s["rk_exp"], d + 1)
                        for j, (x, y) in enumerate(((kk[:, :], exc[:, d]), (r, inc[:, d]))):
                            dve.tensor_tensor(AR[:, d, :, j, :], x.rearrange("p (t n) -> p t n", n=P), y.rearrange("p (t n) -> p t n", n=P), ALU.mult).then_inc(s["rk_ab"], 1)
                        dve.tensor_tensor(BK[:, d, 0], sa[:, d], cum[:, d], ALU.mult)
                        dve.tensor_tensor(BK[:, d, 1], kd[:, d], cum[:, d], ALU.mult).then_inc(s["rk_bk"], 1)
                    dve.wait_ge(s["rk_yact"], 1)
                    link(dve.tensor_tensor(bonus[:, :], bonus[:, :], v, ALU.mult))
                    for t in range(TT):
                        for i, dh in enumerate(TABLE_ORDER):
                            dve.wait_ge(s["rk_gmm"], 4 * t + i + 1)
                            dve.tensor_tensor(G[:, t, dh], m.bank[4 * (t % 2) + dh][:, :], gm[:, dh // 2], ALU.mult).then_inc(s["rk_gsb2"], 1)
                        dve.wait_ge(s["rk_gsb2"], 4 * t + 4)
                        dve.wait_ge(s["rk_lt"], t + 1)
                        for d in range(2):
                            hh = slice(2 * d, 2 * d + 2)
                            dve.tensor_tensor(tm[:, 0, hh], G[:, t, hh, 0:P], lm[:, 0, d].unsqueeze(1).broadcast_to([P, 2, P]), ALU.mult)
                            ins = dve.tensor_tensor(tm[:, 1, hh], m.bank[4 * (t % 2)][:, 2 * d * P:2 * (d + 1) * P].rearrange("p (a b) -> p a b", a=2),
                                                    lm[:, 0, 1 - d].unsqueeze(1).broadcast_to([P, 2, P]), ALU.mult)
                        link(ins)
                        dve.tensor_tensor(XT[:, t], i4, tm[:, 0], ALU.subtract)
                        dve.tensor_tensor(X[:, t], i4, tm[:, 1], ALU.subtract).then_inc(s["rk_xt"], 1)
                        dve.wait_ge(s["rk_xt"], t + 1)
                    for n in range(UNITS):
                        dve.wait_ge(s["rk_t2t"], n + 1)
                        dve.tensor_tensor(XT[:, n % TT], XT[:, n % TT], m.bank[(7, 0)[n % 2]][:, :].rearrange("p (a b) -> p a b", a=4), ALU.subtract).then_inc(s["rk_xt"], 1)
                    dve.wait_ge(s["rk_state"], 64)
                    for n, (g, c) in enumerate(STEPS):
                        dve.wait_ge(s["rk_umm"], n + 1)
                        if n >= 2:
                            dve.wait_ge(s["rk_ymm"], n - 1)
                        for d in range(2):
                            t, half, ch = place(g, c, d)
                            dve.tensor_scalar(Um[:, n % 2, d], m.bank[2 + n % 2][:, d * P:(d + 1) * P], hm[:, 2 + half:3 + half], None, ALU.mult).then_inc(s["rk_usb"], 1)
                        dve.wait_ge(s["rk_smm"], n + 1)
                        for d in range(2):
                            t, half, ch = place(g, c, d)
                            ins = dve.scalar_tensor_tensor(sup[:, d], m.bank[4 + n % 2][:, d * P:(d + 1) * P], wend[:, d, ch:ch + 1], bd[:, :], ALU.mult, ALU.mult)
                        link(ins)
                        dve.wait_ge(s["rk_rs"], n + 1)
                        for d in range(2):
                            t, half, ch = place(g, c, d)
                            dve.scalar_tensor_tensor(st[:, g, d], st[:, g, d], wend[:, d, ch:ch + 1], sup[:, d], ALU.mult, ALU.add).then_inc(s["rk_s"], 1)
                    dve.wait_ge(s["rk_ysb"], 2 * len(STEPS))
                    link(dve.tensor_tensor(Y[:, 0], Y[:, 0], Y[:, 1], ALU.add))
                    yh = Y[:, 0].rearrange("p t (h i) -> p (t h) i", h=2)
                    y2 = Y[:, 1].rearrange("p t (h i) -> p (t h) i", h=2)
                    wide = [P, TT * 2, HS]
                    link(dve.tensor_reduce(stat[:, 0], yh, mybir.AxisListType.X, ALU.add))
                    link(dve.tensor_scalar(stat[:, 0], stat[:, 0], 1.0 / HS, None, ALU.mult))
                    link(dve.tensor_tensor(yh, yh, stat[:, 0].unsqueeze(2).broadcast_to(wide), ALU.subtract))
                    link(dve.tensor_tensor(y2, yh, yh, ALU.mult))
                    dve.tensor_reduce(stat[:, 1], y2, mybir.AxisListType.X, ALU.add).then_inc(s["rk_gn"], 1)
                    dve.wait_ge(s["rk_gnsd"], 1)
                    link(dve.reciprocal(stat[:, 3], stat[:, 2]))
                    dve.tensor_tensor(yh, yh, stat[:, 3].unsqueeze(2).broadcast_to(wide), ALU.mult).then_inc(s["rk_yn"], 1)
                    dve.wait_ge(s["rk_yact"], 2)
                    link(dve.tensor_tensor(bonus[:, :], bonus[:, :], kk[:, :], ALU.add))
                    dve.tensor_tensor(m.yT[:, bass.ds(f, 1), :].squeeze(1), bonus[:, :], gT[:, :], ALU.mult).then_inc(s["rk_out"], 1)
                    dve.wait_ge(s["rk_out"], 1)

        with nc.Fori(0, PAIRS - 1) as f:
            turn(f, True)
            clear(nc, s)
        turn(PAIRS - 1, False)
        with nc.Block() as block:
            @block.sync
            def _(sp):
                sp.dma_start(m.x[:, :, :], m.tokens).then_inc(tab["rt_back"], 16)
                sp.wait_ge(tab["rt_back"], 16)


def fourier_branch(nc, m, L):
    with ExitStack() as ctx:
        fw = buf(ctx, nc, "fw", P, 2, P)
        ft = buf(ctx, nc, "ft", P, TT, 2, T_LAT)
        q = buf(ctx, nc, "fq", P, 2, TT, 2, P)
        s = sems(ctx, nc, "ff_tab", "ff_mm", "ff_q", "ff_y", "ff_out")
        with nc.Block() as block:
            @block.sync
            def _(sp):
                sp.dma_start(fw[:, :, :], m.i["four_w"]).then_inc(s["ff_tab"], 16)
                sp.dma_start(ft[:, :, :, :], m.i["four_t"]).then_inc(s["ff_tab"], 16)

            @block.tensor
            def _(pe):
                pe.wait_ge(s["ff_tab"], 32)
                for n in range(2 * TT):
                    ftile, t = n // TT, n % TT
                    if n >= 4:
                        pe.wait_ge(s["ff_q"], n - 3)
                    pe.matmul(m.bank[n % 4][:, 0:2 * P], L.zf[:, ftile, t * P:(t + 1) * P], fw[:, :, :].rearrange("p a b -> p (a b)"),
                              start=True, stop=True).then_inc(s["ff_mm"], 1)
                pe.wait_ge(s["ff_q"], 2 * TT)
                for ftile in range(2):
                    for c, a, n in SEGS:
                        tiles = [0] if c == 0 else [1, 2, 3, 4]
                        for t in tiles:
                            for j in range(2):
                                mm = pe.matmul(m.bank[4 + 2 * ftile + c][:, 0:n], q[:, ftile, t, j], ft[:, t, j, 0:n],
                                               start=(t == tiles[0] and j == 0), stop=(t == tiles[-1] and j == 1))
                        mm.then_inc(s["ff_y"], 1)

            @block.scalar
            def _(act):
                for n in range(2 * TT):
                    act.wait_ge(s["ff_mm"], n + 1)
                    act.activation(q[:, n // TT, n % TT].rearrange("p a b -> p (a b)"), m.bank[n % 4][:, 0:2 * P], ACT.Copy).then_inc(s["ff_q"], 1)
                for ftile in range(2):
                    for c, a, n in SEGS:
                        act.wait_ge(s["ff_y"], 2 * ftile + c + 1)
                        act.activation(m.yT[:, PAIRS + ftile, a:a + n], m.bank[4 + 2 * ftile + c][:, 0:n], ACT.Copy).then_inc(s["ff_out"], 1)
                act.wait_ge(s["ff_out"], 4)


def rwkv_fourier_layer(nc, m):
    norm_modulate(nc, m, 0, 0)
    with ExitStack() as ctx:
        m.yT = buf(ctx, nc, "yT", P, KD, T)
        with ExitStack() as inner:
            L = Shared()
            L.zw, L.za, L.zg = (buf(inner, nc, n, P, T) for n in ("zw", "za", "zg"))
            with ExitStack() as fourier:
                L.zf = buf(fourier, nc, "zf", P, 2, T)
                lora_and_fourier_inputs(nc, m, L)
                fourier_branch(nc, m, L)
            rwkv_pairs(nc, m, L)
        add_and_norm(nc, m, 0, 0, w_out=m.i["ab_w_out"])


def scan_masks():
    s, t = np.arange(P)[:, None], np.arange(P)[None, :]
    same = s // CH == t // CH
    strict, incl = [same & (s < t), same & (s > t)], [same & (s <= t), same & (s >= t)]
    gmask = np.stack([np.concatenate([strict[d], incl[d], strict[d], incl[d]], 1) for d in range(2)], 1)
    late = lambda i, n: i % (2 * n) >= n
    level = lambda n, d: (s // (2 * n) == t // (2 * n)) & ((late(t, n) & ~late(s, n)) if d == 0 else (late(s, n) & ~late(t, n)))
    lmask = np.stack([np.stack([level(2 ** k, d) for d in range(2)], 1) for k in range(LEVELS)], 1)
    return gmask, lmask


def mixer_constants():
    gmask, lmask = scan_masks()
    c = {"gmask": gmask, "lmask": lmask}
    c["reset"] = np.tile((np.arange(T) % CH != 0), (P, 1))
    c["bd"] = np.kron(np.eye(2), np.ones((CH, CH)))
    first = np.arange(P) < CH
    c["hm"] = np.stack([first, ~first, -1.0 * first, -1.0 * ~first], 1)
    w = 2 * np.pi / HS * np.outer(np.arange(HS), np.arange(HS))
    c["four_w"] = np.stack([np.kron(np.eye(2), np.cos(w)), np.kron(np.eye(2), np.sin(w))], 1) / np.sqrt(HS)
    ft = np.zeros((P, TT, 2, T_LAT))
    for cond, a, n in SEGS:
        w = 2 * np.pi / n * (np.outer(np.arange(n), np.arange(n)) % n)
        for j, table in enumerate((np.cos(w), -np.sin(w))):
            ft[:, a // P:(a + n) // P, j, 0:n] = (table / np.sqrt(n)).reshape(n // P, P, n).transpose(1, 0, 2)
    c["four_t"] = ft
    return c


def mixer_arrays(a):
    DR = HEADS * HS
    wt = a["ab_w_in"].reshape(KD, P, 23, P).transpose(2, 1, 0, 3)
    mu = a["ab_mu"].reshape(21, P)
    col = lambda n: a[n].reshape(PAIRS, P)
    cols = [mu[0:6], mu[6:12], mu[12:18], col("rwkv_k_k"), col("rwkv_k_a"), col("rwkv_r_k"), col("rwkv_gn_g"), col("rwkv_gn_b")]
    cols += [a[n].reshape(2, PAIRS, P)[d] for n in ("rwkv_w0", "rwkv_a0") for d in range(2)]
    lora = [a["rwkv_w2"].reshape(P, PAIRS, P), a["rwkv_a2"].reshape(P, PAIRS, P), a["rwkv_g2"].reshape(P, PAIRS, P)]
    states = np.stack([a["state_rwkv_fwd"], a["state_rwkv_bwd"]]).reshape(2, PAIRS, 2, HS, HS)
    return {
        "w_rkv": np.stack([wt[0:6], wt[6:12], wt[12:18]], 2).reshape(PAIRS, P, 3, KD, P),
        "w_rest": wt[18:23].transpose(1, 0, 2, 3),
        "mu_rest": mu[18:21].T,
        "pcol": np.stack(cols, -1),
        "lora_w": np.stack(lora, 2).transpose(1, 0, 2, 3),
        "state": states.transpose(1, 0, 2, 4, 3),
        "ab_w_out": a["ab_w_out"].reshape(D, D),
    } | hyena_arrays(a)




HY_ORDER, HY_BANDS = 64, 16
HY_EMB = 2 * HY_BANDS + 1
ROUND = float(1.5 * 2 ** 23)
TWO_PI_HI = 6.28125
TWO_PI_LO = float(2 * np.pi - 6.28125)
PI = float(np.float32(np.pi)) - 2e-7
HC_TAPS, HC_BIAS, HC_SKIP, NHC = 0, 9, 12, 13


def hyena_inputs(nc, m, H):
    with ExitStack() as ctx:
        w = buf(ctx, nc, "w_hy", P, 2, 3, KD, P)
        cols = buf(ctx, nc, "hy_cols", P, KD, NHC)
        zp = buf(ctx, nc, "zp_hy", P, 3, ZW)
        c1 = buf(ctx, nc, "conv", P, 3, T)
        us = buf(ctx, nc, "u_turn", P, 2, T)
        c0 = sems(ctx, nc, "hi_cols", "hi_zero", "hi_pre")
        with nc.Block() as block:
            @block.sync
            def _(sp):
                sp.dma_start(cols[:, :, :], m.i["hy_cols"]).then_inc(c0["hi_cols"], 16)
                sp.wait_ge(c0["hi_cols"], 16)
                sp.dma_start(w[:, 0], m.i["hy_w_in"][0]).then_inc(c0["hi_pre"], 16)
                sp.wait_ge(c0["hi_pre"], 16)

            @block.gpsimd
            def _(pool):
                pool.memset(zp[:, :, :], 0.0).then_inc(c0["hi_zero"], 1)
                pool.wait_ge(c0["hi_zero"], 1)
        s = sems(ctx, nc, "hi_w0", "hi_w1", "hi_mm", "hi_zp", "hi_chain", "hi_conv", "hi_u", "hi_tr", "hi_ut")
        with nc.Fori(0, KD // 2) as pair:
            with nc.Block() as block:
                @block.sync
                def _(sp):
                    sp.dma_start(w[:, 1], m.i["hy_w_in"][bass.ds(2 * pair + 1, 1)].squeeze(0)).then_inc(s["hi_w1"], 16)
                    sp.wait_ge(s["hi_mm"], 3)
                    sp.dma_start(w[:, 0], m.i["hy_w_in"][bass.ds(2 * pair + 2, 1)].squeeze(0)).then_inc(s["hi_w0"], 16)
                    sp.wait_ge(s["hi_w0"], 16)

                @block.tensor
                def _(pe):
                    for d in range(2):
                        if d == 1:
                            pe.wait_ge(s["hi_w1"], 16)
                        for q in range(3):
                            if d == 1:
                                pe.wait_ge(s["hi_zp"], q + 1)
                            project_shifted(pe, m, w[:, d], q, s["hi_mm"])
                    for d in range(2):
                        pe.wait_ge(s["hi_u"], d + 1)
                        if d == 1:
                            pe.wait_ge(s["hi_ut"], 1)
                        for t in range(TT):
                            mm = pe.transpose(m.bank[6 + t // 4][:, (t % 4) * P:(t % 4 + 1) * P], us[:, d, t * P:(t + 1) * P], m.ident[:, :])
                        mm.then_inc(s["hi_tr"], 1)

                @block.scalar
                def _(act):
                    for d in range(2):
                        for q in range(3):
                            act.wait_ge(s["hi_mm"], 3 * d + q + 1)
                            if d == 1:
                                act.wait_ge(s["hi_conv"], q + 1)
                            to_padded(act, m, zp, q, s["hi_zp"])
                    for d in range(2):
                        act.wait_ge(s["hi_u"], d + 1)
                        act.activation(pick(H.u[:, :, :], 2 * pair + d), us[:, d], ACT.Copy)
                        act.wait_ge(s["hi_tr"], d + 1)
                        col = bass.ds((2 * pair + d) * P, P)
                        act.activation(H.ut[:, 0:4, col], m.bank[6][:, :].rearrange("p (t n) -> p t n", t=4), ACT.Copy)
                        act.activation(H.ut[:, 4:5, col], m.bank[7][:, 0:P].rearrange("p (t n) -> p t n", t=1), ACT.Copy).then_inc(s["hi_ut"], 1)
                    act.wait_ge(s["hi_ut"], 2)

                @block.vector
                def _(dve):
                    link = linker(dve, s["hi_chain"])
                    for d in range(2):
                        tile = 2 * pair + d
                        col = lambda n: pick(cols[:, :, n:n + 1], tile)
                        for q in range(3):
                            dve.wait_ge(s["hi_zp"], 3 * d + q + 1)
                            for step, (off, n) in enumerate(((0, 1), (-1, 0), (1, 2))):
                                for c, a, width in SEGS:
                                    z = ZOFF[c] + off
                                    src, tap = zp[:, q, z:z + width], col(HC_TAPS + 3 * q + n)
                                    dst = c1[:, q, a:a + width]
                                    if step == 0:
                                        ins = dve.tensor_scalar(dst, src, tap, col(HC_BIAS + q), ALU.mult, ALU.add)
                                    elif step == 2 and q == 0:
                                        ins = dve.scalar_tensor_tensor(H.x0[:, bass.ds(tile, 1), a:a + width].squeeze(1), src, tap, dst, ALU.mult, ALU.add)
                                    else:
                                        ins = dve.scalar_tensor_tensor(dst, src, tap, dst, ALU.mult, ALU.add)
                                    if step < 2 or c == 0:
                                        link(ins)
                            ins.then_inc(s["hi_conv"], 1)
                            dve.wait_ge(s["hi_conv"], 3 * d + q + 1)
                        dve.tensor_tensor(us[:, d], c1[:, 1], c1[:, 2], ALU.mult).then_inc(s["hi_u"], 1)
                        dve.wait_ge(s["hi_u"], d + 1)
            clear(nc, s)


def hyena_filters(nc, m, H):
    with ExitStack() as ctx:
        feats = buf(ctx, nc, "feats", HY_EMB, T)
        w1 = buf(ctx, nc, "hw1", HY_EMB, HY_ORDER)
        w2 = buf(ctx, nc, "hw2", HY_ORDER, HY_ORDER)
        w3 = buf(ctx, nc, "hw3", HY_ORDER, 2 * D)
        hc = buf(ctx, nc, "hcol", HY_ORDER, 3)
        arg = buf(ctx, nc, "arg", HY_ORDER, T)
        whole = buf(ctx, nc, "whole", HY_ORDER, T)
        hid = buf(ctx, nc, "hid", HY_ORDER, 2, T)
        dec = buf(ctx, nc, "dec", P, 2 * D)
        tn = buf(ctx, nc, "tn", P, TT, 2)
        E = m.hT[:, :, :].rearrange("p k t -> p (k t)")[:, 0:4 * D].rearrange("p (a d) -> p a d", a=2)
        hf = buf(ctx, nc, "hf", P, 2, BANK)
        hb = buf(ctx, nc, "hb", P, 2, BANK)
        s = sems(ctx, nc, "hf_in", "hf_mm", "hf_chain", "hf_arg", "hf_sin", "hf_abs", "hf_e", "hf_f", "hf_p", "hf_w", "hf_dve")
        with nc.Block() as block:
            @block.sync
            def _(sp):
                for dst, src in ((feats, m.i["hy_feats"]), (w1, m.i["hy_w1"]), (w2, m.i["hy_w2"]), (w3, m.i["hy_w3"]), (hc, m.i["hy_hcol"]), (tn, m.i["hy_tn"]),
                                 (dec, m.i["hy_decay"].partition_broadcast(P))):
                    sp.dma_start(dst[:], src).then_inc(s["hf_in"], 16)

            @block.tensor
            def _(pe):
                pe.wait_ge(s["hf_in"], 7 * 16)
                for layer, (wt, x) in enumerate(((w1, feats), (w2, hid[:, 0]))):
                    if layer == 1:
                        pe.wait_ge(s["hf_sin"], 1)
                    for c, a, n in SEGS:
                        mm = pe.matmul(m.bank[c][0:HY_ORDER, 0:n], wt[:, :], x[:, a:a + n], start=True, stop=True)
                    mm.then_inc(s["hf_mm"], 1)
                pe.wait_ge(s["hf_sin"], 2)
                for t in range(TT):
                    for c in range(2):
                        n = 2 * t + c
                        if n >= 2:
                            pe.wait_ge(s["hf_p"], 4 * (n - 1))
                        for d in range(2):
                            b = 2 + 2 * (n % 2) + d
                            pe.matmul(m.bank[b][:, :], hid[:, 1, t * P:(t + 1) * P], w3[:, d * D + c * BANK:d * D + (c + 1) * BANK],
                                      start=True, stop=True).then_inc(s["hf_f"], 1)

            @block.scalar
            def _(act):
                act.wait_ge(s["hf_in"], 7 * 16)
                act.activation(dec[:, :], dec[:, :], ACT.Abs).then_inc(s["hf_abs"], 1)
                for layer in range(2):
                    act.wait_ge(s["hf_arg"], layer + 1)
                    act.activation(hid[:, layer], arg[:, :], ACT.Sin).then_inc(s["hf_sin"], 1)
                act.wait_ge(s["hf_abs"], 1)
                for t in range(TT):
                    if t >= 2:
                        act.wait_ge(s["hf_p"], 8 * (t - 1))
                    act.activation(E[:, t % 2], dec[:, :], ACT.Exp, scale=tn[:, t, 0:1]).then_inc(s["hf_e"], 1)

            @block.vector
            def _(dve):
                link = linker(dve, s["hf_chain"])
                dve.wait_ge(s["hf_in"], 7 * 16)
                for layer in range(2):
                    dve.wait_ge(s["hf_mm"], layer + 1)
                    if layer == 1:
                        dve.wait_ge(s["hf_sin"], 1)
                    for c, a, n in SEGS:
                        ins = dve.tensor_scalar(arg[:, a:a + n], m.bank[c][0:HY_ORDER, 0:n], hc[:, layer:layer + 1], hc[:, 2:3], ALU.add, ALU.mult)
                    link(ins)
                    link(dve.tensor_scalar(whole[:, :], arg[:, :], float(1 / (2 * np.pi)), ROUND, ALU.mult, ALU.add))
                    link(dve.tensor_scalar(whole[:, :], whole[:, :], ROUND, None, ALU.subtract))
                    link(dve.scalar_tensor_tensor(arg[:, :], whole[:, :], -TWO_PI_HI, arg[:, :], ALU.mult, ALU.add))
                    link(dve.scalar_tensor_tensor(arg[:, :], whole[:, :], -TWO_PI_LO, arg[:, :], ALU.mult, ALU.add))
                    dve.tensor_scalar(arg[:, :], arg[:, :], PI, -PI, ALU.min, ALU.max).then_inc(s["hf_arg"], 1)
                for t in range(TT):
                    dve.wait_ge(s["hf_e"], t + 1)
                    for c in range(2):
                        n = 2 * t + c
                        b = 2 + 2 * (n % 2)
                        sl = slice(c * BANK, (c + 1) * BANK)
                        dve.wait_ge(s["hf_f"], 2 * n + 2)
                        dve.tensor_tensor(hf[:, n % 2], m.bank[b][:, :], E[:, t % 2, sl], ALU.mult).then_inc(s["hf_p"], 1)
                        dve.scalar_tensor_tensor(hb[:, n % 2], m.bank[b + 1][:, :], tn[:, t, 1:2], E[:, t % 2, D + c * BANK:D + (c + 1) * BANK],
                                                 ALU.mult, ALU.mult).then_inc(s["hf_p"], 1)
                        dve.wait_ge(s["hf_p"], 4 * n + 2)
                        dve.tensor_tensor(H.pm[:, t, 0, sl], hf[:, n % 2], hb[:, n % 2], ALU.add).then_inc(s["hf_p"], 1)
                        dve.tensor_tensor(H.pm[:, t, 1, sl], hf[:, n % 2], hb[:, n % 2], ALU.subtract).then_inc(s["hf_p"], 1)
                dve.wait_ge(s["hf_p"], 8 * TT)


def hyena_spectra(nc, m, H):
    with ExitStack() as ctx:
        tab = buf(ctx, nc, "dft", P, TT, 2, T_LAT)
        tc = buf(ctx, nc, "tc", P, 2, 2, BANK)
        pr = buf(ctx, nc, "pr", P, 4, BANK)
        s = sems(ctx, nc, "hs_tab", "hs_mm", "hs_t", "hs_pr", "hs_y", "hs_read")
        work = [(c, kt, h) for c, a, n in SEGS for kt in range(n // P) for h in range(2)]
        with nc.Block() as block:
            @block.sync
            def _(sp):
                sp.dma_start(tab[:, :, :, :], m.i["dft"]).then_inc(s["hs_tab"], 16)

            @block.tensor
            def _(pe):
                pe.wait_ge(s["hs_tab"], 16)
                for n, (c, kt, h) in enumerate(work):
                    tiles = [0] if c == 0 else [1, 2, 3, 4]
                    sl = slice(h * BANK, (h + 1) * BANK)
                    if n >= 2:
                        pe.wait_ge(s["hs_t"], n - 1)
                        pe.wait_ge(s["hs_read"], n - 1)
                    for b, (j, x) in enumerate(((0, None), (1, None), (0, 0), (1, 1))):
                        for t in tiles:
                            rhs = H.ut[:, t, sl] if x is None else H.pm[:, t, x, sl]
                            mm = pe.matmul(m.bank[4 * (n % 2) + b][:, :], tab[:, t, j, kt * P:(kt + 1) * P], rhs, start=(t == tiles[0]), stop=(t == tiles[-1]))
                    mm.then_inc(s["hs_mm"], 1)

            @block.scalar
            def _(act):
                for n in range(len(work)):
                    act.wait_ge(s["hs_mm"], n + 1)
                    if n >= 2:
                        act.wait_ge(s["hs_read"], n - 1)
                    act.activation(tc[:, n % 2, 0], m.bank[4 * (n % 2) + 2][:, :], ACT.Copy)
                    act.activation(tc[:, n % 2, 1], m.bank[4 * (n % 2) + 3][:, :], ACT.Copy).then_inc(s["hs_t"], 1)

            @block.vector
            def _(dve):
                for n, (c, kt, h) in enumerate(work):
                    dve.wait_ge(s["hs_mm"], n + 1)
                    dve.wait_ge(s["hs_t"], n + 1)
                    if n >= 1:
                        dve.wait_ge(s["hs_y"], 2 * n)
                    b = 4 * (n % 2)
                    dve.tensor_tensor(pr[:, 0], m.bank[b][:, :], tc[:, n % 2, 0], ALU.mult)
                    dve.tensor_tensor(pr[:, 1], m.bank[b + 1][:, :], tc[:, n % 2, 1], ALU.mult)
                    dve.tensor_tensor(pr[:, 2], m.bank[b][:, :], tc[:, n % 2, 1], ALU.mult)
                    dve.tensor_tensor(pr[:, 3], m.bank[b + 1][:, :], tc[:, n % 2, 0], ALU.mult).then_inc(s["hs_read"], 1)
                    dve.wait_ge(s["hs_read"], n + 1)
                    k = kt if c == 0 else 1 + kt
                    sl = slice(h * BANK, (h + 1) * BANK)
                    dve.tensor_tensor(H.y[0][:, k, sl], pr[:, 0], pr[:, 1], ALU.subtract).then_inc(s["hs_y"], 1)
                    dve.tensor_tensor(H.y[1][:, k, sl], pr[:, 2], pr[:, 3], ALU.add).then_inc(s["hs_y"], 1)
                dve.wait_ge(s["hs_y"], 2 * len(work))


def hyena_back(nc, m, H):
    with ExitStack() as ctx:
        tab = buf(ctx, nc, "idft", P, TT, 2, T_LAT)
        cols = buf(ctx, nc, "hy_cols2", P, KD, NHC)
        s = sems(ctx, nc, "hk_tab", "hk_mm", "hk_y", "hk_out")
        with nc.Block() as block:
            @block.sync
            def _(sp):
                sp.dma_start(tab[:, :, :, :], m.i["idft"]).then_inc(s["hk_tab"], 16)
                sp.dma_start(cols[:, :, :], m.i["hy_cols"]).then_inc(s["hk_tab"], 16)

            @block.tensor
            def _(pe):
                pe.wait_ge(s["hk_tab"], 32)
                for k in range(KD):
                    for c, a, n in SEGS:
                        tiles = [0] if c == 0 else [1, 2, 3, 4]
                        i = 2 * k + c
                        if i >= 4:
                            pe.wait_ge(s["hk_y"], i - 3)
                        for t in tiles:
                            for j in range(2):
                                mm = pe.matmul(m.bank[i % 4][:, 0:n], H.y[j][:, t, k * P:(k + 1) * P], tab[:, t, j, 0:n],
                                               start=(t == tiles[0] and j == 0), stop=(t == tiles[-1] and j == 1))
                        mm.then_inc(s["hk_mm"], 1)

            @block.vector
            def _(dve):
                dve.wait_ge(s["hk_tab"], 32)
                for k in range(KD):
                    for c, a, n in SEGS:
                        i = 2 * k + c
                        dve.wait_ge(s["hk_mm"], i + 1)
                        u = H.u[:, k, a:a + n]
                        dve.scalar_tensor_tensor(u, u, cols[:, k, HC_SKIP:HC_SKIP + 1], m.bank[i % 4][:, 0:n], ALU.mult, ALU.add).then_inc(s["hk_y"], 1)
                    dve.wait_ge(s["hk_y"], 2 * k + 2)
                    dve.tensor_tensor(H.u[:, k, :], H.u[:, k, :], H.x0[:, k, :], ALU.mult).then_inc(s["hk_out"], 1)
                dve.wait_ge(s["hk_out"], KD)


def hyena_layer(nc, m):
    norm_modulate(nc, m, 1, 0)
    with ExitStack() as ctx:
        H = Shared()
        H.u = buf(ctx, nc, "u", P, KD, T)
        with ExitStack() as middle:
            H.x0 = buf(middle, nc, "x0", P, KD, T)
            H.y = [m.hT[:, :, :].rearrange("p k t -> p (k t)").rearrange("p (t d) -> p t d", d=D), buf(middle, nc, "y_sin", P, TT, D)]
            with ExitStack() as inner:
                H.ut = buf(inner, nc, "ut", P, TT, D)
                hyena_inputs(nc, m, H)
                H.pm = buf(inner, nc, "pm", P, TT, 2, D)
                hyena_filters(nc, m, H)
                hyena_spectra(nc, m, H)
            hyena_back(nc, m, H)
        m.yT = H.u
        add_and_norm(nc, m, 1, 0, w_out=m.i["hy_w_out"])


def hyena_arrays(a):
    wt = a["hy_w_in"].reshape(KD, P, 3, KD, P).transpose(3, 1, 2, 0, 4)
    taps = a["hy_conv_w"].reshape(3, 3, KD, P)
    bias = a["hy_conv_b"].reshape(3, KD, P)
    cols = [taps[n, q] for q in range(3) for n in range(3)] + [bias[q] for q in range(3)] + [a["hy_skip"].reshape(KD, P)]
    return {
        "hy_w_in": np.concatenate([wt, wt[-1:]], 0),
        "hy_cols": np.stack(cols, -1).transpose(1, 0, 2),
        "hy_w1": a["hy_filt_w1"].reshape(HY_EMB, HY_ORDER), "hy_w2": a["hy_filt_w2"].reshape(HY_ORDER, HY_ORDER),
        "hy_w3": a["hy_filt_w3"].reshape(HY_ORDER, 2 * D),
        "hy_hcol": np.stack([a["hy_filt_b1"].reshape(-1), a["hy_filt_b2"].reshape(-1), a["hy_filt_freq"].reshape(-1)], -1),
        "hy_decay": a["hy_filt_decay"].reshape(2 * D),
        "hy_w_out": a["hy_w_out"].reshape(D, D),
    }


def hyena_constants():
    f32 = np.float32
    feats, tn = [], np.zeros((P, TT, 2))
    dft, idft = np.zeros((P, TT, 2, T_LAT)), np.zeros((P, TT, 2, T_LAT))
    bands = np.linspace(1e-4, HY_BANDS - 1, HY_BANDS, dtype=f32)[None, :]
    for c, a, n in SEGS:
        pos = np.arange(n, dtype=f32)[:, None]
        t = (pos / f32(n - 1)).astype(f32)
        ang = (f32(2.0 * np.pi) * pos / f32(n) * bands).astype(f32).astype(np.float64)
        feats.append(np.concatenate([t, np.cos(ang), -np.sin(ang)], -1))
        tiles = slice(a // P, (a + n) // P)
        tn[:, tiles, 0] = -t.reshape(n // P, P).T
        tn[:, tiles, 1] = (np.arange(n) > 0).reshape(n // P, P).T
        w = np.pi / (2 * n) * (np.outer(np.arange(n), 2 * np.arange(n) + 1) % (4 * n))
        for j, f in enumerate((np.cos(w), np.sin(w))):
            dft[:, tiles, j, 0:n] = f.reshape(n // P, P, n).transpose(1, 0, 2)
            idft[:, tiles, j, 0:n] = (f.T / n).reshape(n // P, P, n).transpose(1, 0, 2)
    return {"hy_feats": np.concatenate(feats, 0).T, "hy_tn": tn, "dft": dft, "idft": idft}


def build(nc, i, o, scratch):
    with ExitStack() as ctx:
        m = Shared()
        m.i, m.o = i, o
        m.mods, m.gates, m.tokens = scratch
        m.x = buf(ctx, nc, "x", P, TT, D)
        m.hT = buf(ctx, nc, "hT", P, KD, T)
        m.modc = buf(ctx, nc, "modc", P, MOD_TILES * 8)
        m.ident = buf(ctx, nc, "ident", P, P)
        m.iota = buf(ctx, nc, "iota", P, P)
        m.eps = buf(ctx, nc, "eps", P, 3)
        m.bank = [ctx.enter_context(nc.psum_tensor(f"bank{b}", [P, BANK], F32)) for b in range(8)]
        load_inputs(nc, m)
        modulation(nc, m)
        rwkv_fourier_layer(nc, m)
        peer(nc, m, 0)
        hyena_layer(nc, m)
        peer(nc, m, 1)
        store_outputs(nc, m)


def constants():
    f32 = np.float32
    quarter = D // 4
    row = np.repeat(np.arange(T_LAT // GRID_W, dtype=f32), GRID_W)
    col = np.tile(np.arange(GRID_W, dtype=f32), T_LAT // GRID_W)
    omega = (1.0 / (f32(10000.0) ** (np.arange(quarter, dtype=f32) / f32(quarter)))).astype(f32)
    ra, ca = (row[:, None] * omega).astype(np.float64), (col[:, None] * omega).astype(np.float64)
    c = {"pos": np.concatenate([np.sin(ra), np.cos(ra), np.sin(ca), np.cos(ca)], -1)}
    c["ident"] = np.eye(P)
    c["iota"] = np.tile(np.arange(P), (P, 1))
    c["eps"] = np.tile(np.array([LN_EPS, GN_EPS, 1e-12]), (P, 1))
    return c


def kernel(**inputs):
    import concourse.bacc as _bacc
    from concourse.bass_utils import run_bass_kernel_spmd as _run

    a = {k: np.asarray(v) for k, v in inputs.items()}
    arr = {
        "x_prompt": a["x_prompt"].reshape(T_CTX, D), "x_sample": a["x_sample"].reshape(T_LAT, D),
        "cond": np.stack([a["c_ctx"], a["c"].reshape(D)], -1).reshape(KD, P, 2).transpose(1, 0, 2),
        "w_mod": a["w_mod"].reshape(DEPTH, KD, P, 12, BANK).transpose(0, 3, 2, 1, 4).reshape(MOD_TILES, P, KD, BANK),
        "b_mod": a["b_mod"].reshape(-1),
        "peer_wq": a["peer_wq"].reshape(DEPTH, KD, P, 16, P).transpose(0, 3, 2, 1, 4),
        "peer_k": np.stack([a["peer_k1"], a["peer_k2"]], 2).transpose(0, 4, 1, 2, 3).reshape(DEPTH, P, 16, P),
        "peer_u": a["peer_u"].reshape(DEPTH, P, P, KD, P).transpose(0, 1, 4, 3, 2),
        "peer_v": a["peer_v"].reshape(DEPTH, P, P, D),
    }
    for n in ("ln_mix_g", "ln_mix_b", "ln_ffn_g", "ln_ffn_b"):
        arr[n] = a[n]
    arr |= mixer_arrays(a)
    arr |= {k: v.astype(np.float32) for k, v in (constants() | mixer_constants() | hyena_constants()).items()}
    arr = {k: np.ascontiguousarray(v) for k, v in arr.items()}
    nc = _bacc.Bacc("TRN2", target_bir_lowering=False, num_devices=1)
    i = {k: nc.dram_tensor(f"in_{k}", v.shape, F32, kind="ExternalInput").ap() for k, v in arr.items()}
    shapes = {"y_prompt": (T_CTX, D), "y_sample": (T_LAT, D), "states": (PAIRS, 2, 2, HS, HS)}
    o = {k: nc.dram_tensor(f"out_{k}", s, F32, kind="ExternalOutput").ap() for k, s in shapes.items()}
    scratch = [nc.dram_tensor(n, s, F32, kind="Internal").ap()
               for n, s in (("mods", (2, MOD_TILES * BANK)), ("gates", (NKEY, NKEY, T)), ("tokens", (P, TT, D)))]
    build(nc, i, o, scratch)
    r = _run(nc, [{f"in_{k}": v for k, v in arr.items()}], core_ids=[0]).results[0]
    st = r["out_states"].transpose(1, 0, 2, 4, 3).reshape(2, 1, 1, HEADS, HS, HS)
    return r["out_y_prompt"].reshape(1, T_CTX, D), r["out_y_sample"].reshape(1, T_LAT, D), st[0], st[1]
```
